# Optimizing a Trainium2 kernel written in Bass

```python
import math
import jax, jax.numpy as jnp
from jax import lax
import numpy as np

D_MODEL = 1024
BATCH = 1
SEQ = 512
DEPTH = 2

CHUNK = 64
EPS = 1e-6
ATT_HEAD_DIM = 64
ATT_Q_HEADS = 8
ATT_KV_HEADS = 2
ATT_GROUP = ATT_Q_HEADS // ATT_KV_HEADS
WINDOW = 128
SGU_BLOCK = 128
SGU_GROUPS = 8
SGU_GROUP_DIM = 64
SGU_WIDTH = SGU_GROUPS * SGU_GROUP_DIM
Q_W = ATT_Q_HEADS * ATT_HEAD_DIM
KV_W = ATT_KV_HEADS * ATT_HEAD_DIM
IN_W = Q_W + 2 * KV_W + 2 * SGU_WIDTH
MIX_W = Q_W + SGU_WIDTH
D_FF = 4 * D_MODEL

kernel_name = "hybrid_swa_sink_alibi_gmlp_block"

def rms_norm(x, g):
    xf = x.astype(jnp.float32)
    y = xf * lax.rsqrt(jnp.mean(xf * xf, axis=-1, keepdims=True) + EPS)
    return (y * g.astype(jnp.float32)).astype(x.dtype)

def alibi_slopes(n_heads):
    h = jnp.arange(1, n_heads + 1, dtype=jnp.float32)
    return jnp.exp2(-8.0 * h / n_heads)

def window_attention(q, k, v, sinks):
    B, S = q.shape[0], q.shape[1]
    nc = S // CHUNK
    qb = q.reshape(B, nc, CHUNK, ATT_KV_HEADS, ATT_GROUP, ATT_HEAD_DIM)

    def band(t):
        tc = t.reshape(B, nc, CHUNK, ATT_KV_HEADS, ATT_HEAD_DIM)
        prev = jnp.pad(tc, ((0, 0), (1, 0), (0, 0), (0, 0), (0, 0)))[:, :-1]
        return jnp.concatenate([prev, tc], axis=2)

    kb, vb = band(k), band(v)
    s = jnp.einsum('bnqhgd,bnkhd->bnhgqk', qb, kb).astype(jnp.float32)
    s = s * (ATT_HEAD_DIM ** -0.5)
    qi = jnp.arange(CHUNK)[:, None]
    kj = jnp.arange(2 * CHUNK)[None, :]
    dist = jnp.abs(qi + CHUNK - kj).astype(jnp.float32)
    slopes = alibi_slopes(ATT_Q_HEADS).reshape(ATT_KV_HEADS, ATT_GROUP)
    s = s - slopes[:, :, None, None] * dist
    valid = (jnp.arange(nc)[:, None] > 0) | (kj >= CHUNK)
    s = jnp.where(valid[None, :, None, None, None, :], s, jnp.finfo(jnp.float32).min)
    sink = sinks.astype(jnp.float32).reshape(ATT_KV_HEADS, ATT_GROUP)[None, None, :, :, None]
    lse = jnp.logaddexp(jax.nn.logsumexp(s, axis=-1), sink)
    p = jnp.exp(s - lse[..., None]).astype(v.dtype)
    o = jnp.einsum('bnhgqk,bnkhd->bnqhgd', p, vb)
    return o.reshape(B, S, Q_W)

def spatial_gating(u, v, w_s, b_s):
    B, S = u.shape[0], u.shape[1]
    nb = S // SGU_BLOCK
    vf = v.astype(jnp.float32).reshape(B, nb, SGU_BLOCK, SGU_GROUPS, SGU_GROUP_DIM)
    mu = jnp.mean(vf, axis=-1, keepdims=True)
    var = jnp.mean(jnp.square(vf - mu), axis=-1, keepdims=True)
    vn = ((vf - mu) * lax.rsqrt(var + EPS)).astype(v.dtype)
    pos = jnp.arange(SGU_BLOCK) // CHUNK
    mask = (pos[:, None] >= pos[None, :]).astype(w_s.dtype)
    w = w_s * mask[None]
    s = jnp.einsum('gij,bnjgc->bnigc', w, vn) + b_s.T[:, :, None]
    return u * s.reshape(B, S, SGU_WIDTH)

def setup_inputs(seed: int = 0) -> dict:
    key = jax.random.key(seed)
    ks = jax.random.split(key, 12)
    f32 = jnp.float32
    x = jax.random.normal(ks[0], (BATCH, SEQ, D_MODEL), f32)
    norm_mix = 1.0 + 0.05 * jax.random.normal(ks[1], (DEPTH, D_MODEL), f32)
    w_in = jax.random.normal(ks[2], (DEPTH, D_MODEL, IN_W), f32) * D_MODEL ** -0.5
    sinks = 0.5 * jax.random.normal(ks[3], (DEPTH, ATT_Q_HEADS), f32)
    w_s = jax.random.normal(ks[4], (DEPTH, SGU_GROUPS, SGU_BLOCK, SGU_BLOCK), f32) * SGU_BLOCK ** -0.5
    b_s = 1.0 + 0.1 * jax.random.normal(ks[5], (DEPTH, SGU_GROUPS, SGU_BLOCK), f32)
    w_o = jax.random.normal(ks[6], (DEPTH, MIX_W, D_MODEL), f32) * MIX_W ** -0.5
    norm_ffn = 1.0 + 0.05 * jax.random.normal(ks[7], (DEPTH, D_MODEL), f32)
    w_up = jax.random.normal(ks[8], (DEPTH, D_MODEL, D_FF), f32) * D_MODEL ** -0.5
    w_down = jax.random.normal(ks[9], (DEPTH, D_FF, D_MODEL), f32) * D_FF ** -0.5
    norm_final = 1.0 + 0.05 * jax.random.normal(ks[10], (D_MODEL,), f32)
    return {"x": x, "norm_mix": norm_mix, "w_in": w_in, "sinks": sinks,
            "w_s": w_s, "b_s": b_s, "w_o": w_o, "norm_ffn": norm_ffn,
            "w_up": w_up, "w_down": w_down, "norm_final": norm_final}

def reference(x, norm_mix, w_in, sinks, w_s, b_s, w_o, norm_ffn, w_up, w_down, norm_final):
    B, S = x.shape[0], x.shape[1]
    for l in range(DEPTH):
        h = rms_norm(x, norm_mix[l])
        proj = h @ w_in[l]
        q = proj[..., :Q_W].reshape(B, S, ATT_Q_HEADS, ATT_HEAD_DIM)
        k = proj[..., Q_W:Q_W + KV_W].reshape(B, S, ATT_KV_HEADS, ATT_HEAD_DIM)
        v = proj[..., Q_W + KV_W:Q_W + 2 * KV_W].reshape(B, S, ATT_KV_HEADS, ATT_HEAD_DIM)
        uv = jax.nn.gelu(proj[..., Q_W + 2 * KV_W:])
        u, gv = uv[..., :SGU_WIDTH], uv[..., SGU_WIDTH:]
        att = window_attention(q, k, v, sinks[l])
        sgu = spatial_gating(u, gv, w_s[l], b_s[l])
        x = x + jnp.concatenate([att, sgu], axis=-1) @ w_o[l]
        h = rms_norm(x, norm_ffn[l])
        x = x + jnp.square(jax.nn.relu(h @ w_up[l])) @ w_down[l]
    return rms_norm(x, norm_final)


_drawn_inputs = setup_inputs


def setup_inputs(seed=0):
    import zlib

    import numpy as np

    out = dict(_drawn_inputs(seed))
    spreads = {}
    factors = {'sinks': 6.901}
    for name, (base, spread) in spreads.items():
        noise = np.random.default_rng([zlib.crc32(name.encode()), seed]).standard_normal(out[name].shape)
        drawn = base * np.exp(spread * noise) if base else spread * noise
        out[name] = __import__('jax').numpy.asarray(drawn.astype(out[name].dtype))
    for name, factor in factors.items():
        out[name] = (out[name] * factor).astype(out[name].dtype)
    return out
```

```python
from contextlib import ExitStack

import concourse.bass as bass
from concourse import mybir

F32 = mybir.dt.float32
F32R = mybir.dt.float32r
ALU = mybir.AluOpType
ACT = mybir.ActivationFunctionType
AX = mybir.AxisListType

P = 128
DEPTH = 2
SEQ = 512
D = 1024
KC = D // P
CHUNK = 64
NCH = SEQ // CHUNK
HD = 64
HQ = 8
NTOK = SEQ // P
GROUPS = 8
FF = 4 * D
QUARTERS = FF // D
EPS = 1e-6
GELU_C = 0.7978845608028654
GELU_A = 0.044715
LOWEST = -3.4028234663852886e38

K_POS, V_POS, Q_POS, GV_POS, U_POS, WO_POS, MLP_POS = 0, 1, 2, 6, 10, 14, 22
PER_QUARTER = 2 * KC
PER_LAYER = MLP_POS + QUARTERS * PER_QUARTER
SLOTS = 4
BANKS = 4
CREDIT = 4
BY_POOL = 3


def slot_of(pos):
    return pos % SLOTS if pos < MLP_POS else (pos - MLP_POS) % SLOTS


SLOT_USES = [sum(slot_of(i) == s for i in range(PER_LAYER)) for s in range(SLOTS)]


def landed_value(layer, pos):
    s = slot_of(pos)
    before = sum(slot_of(i) == s for i in range(pos))
    return (layer * SLOT_USES[s] + before + 1) * 16


def mlp_landed_value(layer, quad, s):
    before = sum(slot_of(i) == s for i in range(MLP_POS))
    return (layer * SLOT_USES[s] + before + quad + 1) * 16


def before_in_slot(pos):
    s = slot_of(pos)
    back = [i for i in range(pos) if slot_of(i) == s]
    return back[-1] if back else max(i for i in range(PER_LAYER) if slot_of(i) == s) - PER_LAYER


FM_PER_LAYER = PER_LAYER - 4


def fm_of(pos):
    return pos if pos < GV_POS else pos - 4


def before_in_bank(fm):
    if fm >= BANKS:
        return fm - BANKS
    return max(j for j in range(FM_PER_LAYER) if j % BANKS == fm) - FM_PER_LAYER


def build(nc, x, gains, weights, sinks, ws, bs, alibi, ident_in, out):
    with ExitStack() as ctx:
        def sb(name, shape, dt=F32):
            return ctx.enter_context(nc.sbuf_tensor(name, shape, dt))

        def sem(name):
            return ctx.enter_context(nc.semaphore(name))

        raw = sb("raw", [P, SLOTS, D])
        whi = sb("whi", [P, SLOTS, D], F32R)
        wlo = sb("wlo", [P, SLOTS, D], F32R)
        xt = sb("xt", [P, KC, SEQ])
        xhi = sb("xhi", [P, KC, SEQ], F32R)
        xlo = sb("xlo", [P, KC, SEQ], F32R)
        ahi = sb("ahi", [P, KC, SEQ], F32R)
        alo = sb("alo", [P, KC, SEQ], F32R)
        sumsq = sb("sumsq", [P, SEQ])
        sq = sb("sq", [P, 2, SEQ])
        rbc = sb("rbc", [P, SEQ])
        rcol = sb("rcol", [P, NTOK])
        kt = sb("kt", [P, CHUNK + SEQ])
        vt = sb("vt", [P, CHUNK + SEQ])
        qt = sb("qt", [P, NCH, 4, CHUNK])
        vband = sb("vband", [P, NCH, P])
        band = sb("band", [P, 4, NCH, P])
        negmax = sb("negmax", [P, 4, NCH])
        rowmax = sb("rowmax", [P, 4, NCH])
        sinkarg = sb("sinkarg", [P, 4, NCH])
        sinkexp = sb("sinkexp", [P, 4, NCH])
        den = sb("den", [P, 4, NCH])
        dsum = sb("dsum", [P, 4, NCH])
        rden = sb("rden", [P, 4, NCH])
        ut = sb("ut", [P, 4, SEQ])
        gv = sb("gv", [P, NTOK, SEQ])
        z = sb("z", [P, 2, SEQ])
        pp = sb("pp", [P, 2, SEQ])
        gsum = sb("gsum", [P, NTOK, GROUPS])
        gvar = sb("gvar", [P, NTOK, GROUPS])
        grstd = sb("grstd", [P, NTOK, GROUPS])
        wst = sb("wst", [P, GROUPS, P])
        bsb = sb("bsb", [P, 4, P])
        gain = sb("gain", [P, (2 * DEPTH + 1) * KC])
        sink = sb("sink", [P, DEPTH * 4])
        sink_now = sb("sink_now", [P, 4])
        bias = sb("bias", [P, 4, 2, P])
        ident = sb("ident", [P, P])
        ones = sb("ones", [P, P])
        eps = sb("eps", [P, 2])
        zero = sb("zero", [P, 1])

        bank = [ctx.enter_context(nc.psum_tensor(f"bank{i}", [P, 512], F32)) for i in range(8)]

        raw_landed = [sem(f"raw_landed{s}") for s in range(SLOTS)]
        x_landed = [sem(f"x_landed{m}") for m in range(KC)]
        gain_landed = sem("gain_landed")
        const_landed = sem("const_landed")
        gate_landed = sem("gate_landed")
        zeros_set = sem("zeros_set")
        zero_set = sem("zero_set")
        whi_ready = sem("whi_ready")
        whi_by_pool = sem("whi_by_pool")
        wlo_ready = sem("wlo_ready")
        group_done = sem("group_done")
        evicted = sem("evicted")
        xhi_ready = sem("xhi_ready")
        xlo_ready = sem("xlo_ready")
        sq_ready = sem("sq_ready")
        sumsq_steps = sem("sumsq_steps")
        stat_filled = sem("stat_filled")
        std_ready = sem("std_ready")
        r_ready = sem("r_ready")
        scores_filled = sem("scores_filled")
        scores_taken = sem("scores_taken")
        sink_taken = sem("sink_taken")
        rowmax_ready = sem("rowmax_ready")
        negmax_ready = sem("negmax_ready")
        sinkarg_ready = sem("sinkarg_ready")
        exps_done = sem("exps_done")
        dsum_ready = sem("dsum_ready")
        rden_ready = sem("rden_ready")
        probs_ready = sem("probs_ready")
        vband_filled = sem("vband_filled")
        vband_taken = sem("vband_taken")
        pt_filled = sem("pt_filled")
        pt_taken = sem("pt_taken")
        pv_filled = sem("pv_filled")
        att_hi = sem("att_hi")
        att_lo = sem("att_lo")
        gv_done = sem("gv_done")
        square_ready = sem("square_ready")
        poly_ready = sem("poly_ready")
        tanh_ready = sem("tanh_ready")
        gelu_ready = sem("gelu_ready")
        gsum_ready = sem("gsum_ready")
        centred = sem("centred")
        csq_ready = sem("csq_ready")
        gvar_ready = sem("gvar_ready")
        gstd_ready = sem("gstd_ready")
        grstd_ready = sem("grstd_ready")
        vn_ready = sem("vn_ready")
        sgu_filled = sem("sgu_filled")
        sgu_taken = sem("sgu_taken")
        sgu_ready = sem("sgu_ready")
        sgu_hi = sem("sgu_hi")
        sgu_lo = sem("sgu_lo")
        hid_ready = sem("hid_ready")
        hid_hi = sem("hid_hi")
        hid_lo = sem("hid_lo")
        out_ready = sem("out_ready")
        out_stored = sem("out_stored")

        def group_value(layer, pos):
            return layer * PER_LAYER + (pos + 1 + CREDIT)

        def evicted_value(layer, fm):
            return layer * FM_PER_LAYER + (fm + 1 + CREDIT)

        block = ctx.enter_context(nc.Block())

        @block.sync
        def _(sp):
            def load(layer, pos, group):
                sp.wait_ge(wlo_ready, group_value(layer, before_in_slot(pos)))
                sp.dma_start(raw[:, slot_of(pos), :], weights[bass.ds(group, 1)].rearrange("a p f -> (a p) f")) \
                    .then_inc(raw_landed[slot_of(pos)], 16)

            sp.dma_start(gain[:, :], gains).then_inc(gain_landed, 16)
            with sp.Fori(0, DEPTH) as l:
                for pos in range(MLP_POS):
                    load(l, pos, l * PER_LAYER + pos)
                    if pos == 3:
                        lo, hi = slice(0, CHUNK), slice(CHUNK, P)
                        wl = ws[bass.ds(l, 1)].rearrange("a j g i -> (a j) g i")
                        sp.dma_start(wst[lo, :, :], wl[lo, :, :]).then_inc(gate_landed, 16)
                        sp.dma_start(wst[hi, :, CHUNK:P], wl[hi, :, CHUNK:P]).then_inc(gate_landed, 16)
                        for r in range(2):
                            src = bs[bass.ds(l, 1), r].rearrange("a c i -> a (c i)").broadcast_to([HD, 4 * P])
                            sp.dma_start(bsb[r * HD:(r + 1) * HD, :, :].rearrange("p c i -> p (c i)"), src) \
                                .then_inc(gate_landed, 16)
                with sp.Fori(0, QUARTERS * PER_QUARTER // SLOTS) as quad:
                    for s in range(SLOTS):
                        back = min(MLP_POS + s - before_in_slot(MLP_POS + s), SLOTS)
                        sp.wait_ge(wlo_ready, l * PER_LAYER + quad * SLOTS + (MLP_POS + s - back + 1 + CREDIT))
                        group = l * PER_LAYER + quad * SLOTS + (MLP_POS + s)
                        sp.dma_start(raw[:, s, :], weights[bass.ds(group, 1)].rearrange("a p f -> (a p) f")) \
                            .then_inc(raw_landed[s], 16)
            for m in range(KC):
                sp.wait_ge(out_ready, m + 1)
                sp.dma_start(out[m], band[:, m // 2, (m % 2) * 4:(m % 2) * 4 + 4, :].rearrange("p n k -> p (n k)")) \
                    .then_inc(out_stored, 16)
            sp.wait_ge(out_stored, 16 * KC)

        @block.gpsimd
        def _(pool):
            pool.memset(wst[:, :, :], 0.0).then_inc(zeros_set, 1)
            pool.memset(zero[:, :], 0.0).then_inc(zero_set, 1)
            pool.memset(eps[:, 0:1], EPS).then_inc(zeros_set, 1)
            pool.wait_ge(zero_set, 1)
            pool.memset(eps[:, 1:2], 4 * EPS).then_inc(wlo_ready, CREDIT)

            def low(slot, value):
                pool.tensor_tensor(wlo[:, slot, :], raw[:, slot, :], whi[:, slot, :], ALU.subtract) \
                    .then_inc(wlo_ready, 1)

            with pool.Fori(0, DEPTH) as l:
                for pos in range(MLP_POS):
                    s = slot_of(pos)
                    if pos < BY_POOL:
                        pool.wait_ge(raw_landed[s], landed_value(l, pos))
                        pool.wait_ge(group_done, group_value(l, before_in_slot(pos)))
                        pool.tensor_tensor(whi[:, s, :], raw[:, s, :], zero[:, :].broadcast_to([P, D]), ALU.add) \
                            .then_inc(whi_by_pool, 1)
                        pool.wait_ge(whi_by_pool, l * BY_POOL + (pos + 1))
                    else:
                        pool.wait_ge(whi_ready, l * (PER_LAYER - BY_POOL) + (pos - BY_POOL + 1))
                    low(s, None)
                with pool.Fori(0, QUARTERS * PER_QUARTER // SLOTS) as quad:
                    for s in range(SLOTS):
                        pool.wait_ge(whi_ready, l * (PER_LAYER - BY_POOL) + quad * SLOTS + (MLP_POS + s - BY_POOL + 1))
                        low(s, None)

        @block.tensor
        def _(pe):
            def products(pos, lay, q, hi, lo, before_chunk):
                fm, s = fm_of(pos), slot_of(pos)
                o = bank[fm % BANKS]
                pe.wait_ge(wlo_ready, lay * PER_LAYER + q * PER_QUARTER + (pos + 1 + CREDIT))
                for kc in range(KC):
                    before_chunk(kc)
                    wc = slice(kc * P, (kc + 1) * P)
                    pe.matmul(o[:, :], wlo[:, s, wc], hi[:, kc, :], start=(kc == 0), stop=False)
                    pe.matmul(o[:, :], whi[:, s, wc], hi[:, kc, :], start=False, stop=False)
                    mm = pe.matmul(o[:, :], whi[:, s, wc], lo[:, kc, :], start=False, stop=(kc == KC - 1))
                mm.then_inc(group_done, 1)

            def nothing(kc):
                pass

            def statistics(norm, columns):
                pe.wait_ge(sumsq_steps, norm * (KC - 1) + (KC - 1))
                mm = pe.matmul(bank[4][:, :], ones[:, :], sumsq[:, :], start=True, stop=True)
                if columns:
                    for t in range(NTOK):
                        mm = pe.matmul(bank[5][:, t:t + 1], sumsq[:, t * P:(t + 1) * P], ones[:, 0:1],
                                       start=True, stop=True)
                mm.then_inc(stat_filled, 1)

            def bank_free(lay, fm):
                pe.wait_ge(evicted, evicted_value(lay, before_in_bank(fm)))

            pe.wait_ge(const_landed, 16 * 4)
            with pe.Fori(0, DEPTH) as l:
                for pos in range(GV_POS):
                    bank_free(l, fm_of(pos))
                    if pos == 0:
                        products(pos, l, 0, xhi, xlo,
                                 lambda kc: pe.wait_ge(xlo_ready, l * (2 * KC) + (kc + 1)))
                        statistics(2 * l, True)
                    else:
                        products(pos, l, 0, xhi, xlo, nothing)

                for s4 in range(4):
                    pos = GV_POS + s4
                    s = slot_of(pos)
                    pe.wait_ge(wlo_ready, group_value(l, pos))
                    if s4 == 0:
                        pe.wait_ge(std_ready, 2 * l + 1)
                    for t in range(NTOK):
                        tok = slice(t * P, (t + 1) * P)
                        for b in range(2):
                            kc, wc = 2 * s4 + b, slice(b * 512, (b + 1) * 512)
                            o = bank[4 + t][:, :]
                            pe.matmul(o, xhi[:, kc, tok], wlo[:, s, wc], start=(kc == 0), stop=False)
                            pe.matmul(o, xhi[:, kc, tok], whi[:, s, wc], start=False, stop=False)
                            mm = pe.matmul(o, xlo[:, kc, tok], whi[:, s, wc], start=False, stop=(kc == KC - 1))
                        if s4 == 3 and t < NTOK - 1:
                            mm.then_inc(gv_done, 1)
                    mm.then_inc(group_done, 1)
                    c = s4
                    half, tp = c // 2, c % 2
                    part = slice(half * HD, (half + 1) * HD)
                    if c == 0:
                        pe.wait_ge(evicted, evicted_value(l, Q_POS + 3))
                    for nh in range(2):
                        f = 2 * c + nh
                        if f >= BANKS:
                            pe.wait_ge(scores_taken, l * 8 + (f - BANKS + 1))
                        for n in range(4 * nh, 4 * nh + 4):
                            mm = pe.matmul(bank[(2 + f) % BANKS][:, (n % 4) * P:(n % 4 + 1) * P],
                                           qt[part, n, 2 * tp:2 * tp + 2, :].rearrange("p t q -> p (t q)"),
                                           kt[part, n * CHUNK:n * CHUNK + P], start=True, stop=True)
                        mm.then_inc(scores_filled, 1)

                for nh in range(2):
                    pe.wait_ge(scores_taken, l * 8 + (4 + nh + 1))
                    for n in range(4 * nh, 4 * nh + 4):
                        mm = pe.transpose(bank[2 + nh][:, (n % 4) * P:(n % 4 + 1) * P],
                                          vt[:, n * CHUNK:n * CHUNK + P], ident[:, :])
                    mm.then_inc(vband_filled, 1)

                for c in range(4):
                    pos = U_POS + c
                    if c < 2:
                        pe.wait_ge(vband_taken, l * 2 + (c + 1))
                    else:
                        pe.wait_ge(scores_taken, l * 8 + (6 + c - 2 + 1))
                    products(pos, l, 0, xhi, xlo, nothing)
                    pe.wait_ge(probs_ready, l * 4 + (c + 1))
                    for nh in range(2):
                        f = 2 * c + nh
                        if f < 4:
                            pe.wait_ge(square_ready, l * 8 + (f + 1))
                        else:
                            pe.wait_ge(pt_taken, l * 8 + (f - 4 + 1))
                        for n in range(4 * nh, 4 * nh + 4):
                            mm = pe.transpose(bank[4 + f % 4][:, (n % 4) * P:(n % 4 + 1) * P],
                                              band[:, c, n, :], ident[:, :])
                        mm.then_inc(pt_filled, 1)

                pe.wait_ge(pt_taken, l * 8 + 8)
                pe.wait_ge(vband_taken, l * 2 + 2)
                for b in range(4):
                    for n in range(2 * b, 2 * b + 2):
                        for half in range(2):
                            part = slice(half * HD, (half + 1) * HD)
                            mm = pe.matmul(bank[4 + b][part, (n % 2) * 256:(n % 2 + 1) * 256],
                                           vband[:, n, part], band[:, 2 * half:2 * half + 2, n, :],
                                           start=True, stop=True)
                    mm.then_inc(pv_filled, 1)

                pe.wait_ge(gate_landed, l * 64 + 64)
                pe.wait_ge(vn_ready, l * 4 + 4)
                for pr in range(4):
                    bank_free(l, 10 + pr)
                    for t in range(NTOK):
                        for r in range(2):
                            g = 2 * pr + r
                            mm = pe.matmul(bank[(10 + pr) % BANKS][r * HD:(r + 1) * HD, t * P:(t + 1) * P],
                                           gv[:, t, g * HD:(g + 1) * HD], wst[:, g, :], start=True, stop=True)
                    mm.then_inc(sgu_filled, 1)

                def mixed(kc):
                    if kc == 0:
                        pe.wait_ge(att_lo, l * 4 + 4)
                    if kc >= 4:
                        pe.wait_ge(sgu_lo, l * 4 + (kc - 4 + 1))

                for m in range(KC):
                    pos = WO_POS + m
                    if m < 4:
                        pe.wait_ge(sgu_taken, l * 4 + (m + 1))
                    else:
                        bank_free(l, fm_of(pos))
                    products(pos, l, 0, ahi, alo, mixed if m == 0 else nothing)

                statistics(2 * l + 1, False)

                def quarter(q):
                    for m in range(KC):
                        pos = MLP_POS + m
                        pe.wait_ge(evicted, l * FM_PER_LAYER + q * PER_QUARTER + (fm_of(pos) - BANKS + 1 + CREDIT))
                        products(pos, l, q, xhi, xlo,
                                 (lambda kc: pe.wait_ge(xlo_ready, l * (2 * KC) + (KC + kc + 1)))
                                 if m == 0 else nothing)
                    for m in range(KC):
                        pos = MLP_POS + KC + m
                        pe.wait_ge(evicted, l * FM_PER_LAYER + q * PER_QUARTER + (fm_of(pos) - BANKS + 1 + CREDIT))
                        products(pos, l, q, ahi, alo,
                                 (lambda kc: pe.wait_ge(hid_lo, l * (QUARTERS * KC) + q * KC + (kc + 1)))
                                 if m == 0 else nothing)

                with pe.Fori(0, QUARTERS - 1) as q:
                    quarter(q)
                quarter(QUARTERS - 1)
            statistics(2 * DEPTH, False)

        @block.scalar
        def _(act):
            def high(l, pos, q=0):
                s = slot_of(pos)
                if pos < MLP_POS:
                    act.wait_ge(raw_landed[s], landed_value(l, pos))
                    act.wait_ge(group_done, group_value(l, before_in_slot(pos)))
                else:
                    k = pos - MLP_POS
                    act.wait_ge(raw_landed[s], l * (16 * SLOT_USES[s]) + q * (16 * PER_QUARTER // SLOTS)
                                + mlp_landed_value(0, k // SLOTS, s))
                    act.wait_ge(group_done, l * PER_LAYER + q * PER_QUARTER
                                + (max(before_in_slot(pos), pos - SLOTS) + 1 + CREDIT))
                act.activation(whi[:, s, :], raw[:, s, :], ACT.Copy).then_inc(whi_ready, 1)

            def norm_chunk(norm, m, gain_col):
                act.mul(xhi[:, m, :], xt[:, m, :], gain_col).then_inc(xhi_ready, 1)
                dst = sumsq[:, :] if m == 0 else sq[:, m % 2, :]
                if m >= 3:
                    act.wait_ge(sumsq_steps, norm * (KC - 1) + (m - 2))
                act.activation(dst, xt[:, m, :], ACT.Square).then_inc(sq_ready, 1)

            def std(norm, columns):
                act.wait_ge(stat_filled, norm + 1)
                a = act.activation(rbc[:, :], bank[4][:, :], ACT.Sqrt, scale=1.0 / D, bias=eps[:, 0:1])
                if columns:
                    a = act.activation(rcol[:, :], bank[5][:, 0:NTOK], ACT.Sqrt, scale=1.0 / D, bias=eps[:, 0:1])
                a.then_inc(std_ready, 1)

            for m in range(KC):
                act.dma_start(xt[:, m, :], x[m]).then_inc(x_landed[m], 16)
            act.dma_start(ident[:, :], ident_in).then_inc(const_landed, 16)
            act.dma_start(bias[:, :, :, :].rearrange("p c a k -> p (c a k)"), alibi).then_inc(const_landed, 16)
            for r in range(2):
                src = sinks[:, r].rearrange("(a l) c -> a (l c)", a=1).broadcast_to([HD, DEPTH * 4])
                act.dma_start(sink[r * HD:(r + 1) * HD, :], src).then_inc(const_landed, 16)
            act.wait_ge(gain_landed, 16)
            act.wait_ge(zeros_set, 2)
            act.wait_ge(wlo_ready, CREDIT)
            for m in range(KC):
                act.wait_ge(x_landed[m], 16)
                norm_chunk(0, m, gain[:, m:m + 1])

            with act.Fori(0, DEPTH) as l:
                def softmax(c):
                    act.wait_ge(negmax_ready, l * 4 + (c + 1))
                    for n in range(NCH):
                        act.activation(band[:, c, n, :], band[:, c, n, :], ACT.Exp, bias=negmax[:, c, n:n + 1],
                                       accum_out=den[:, c, n:n + 1])
                    act.wait_ge(sinkarg_ready, l * 4 + (c + 1))
                    act.activation(sinkexp[:, c, :], sinkarg[:, c, :], ACT.Exp).then_inc(exps_done, 1)

                def tanh(k):
                    act.wait_ge(poly_ready, l * 8 + (k + 1))
                    act.activation(pp[:, k % 2, :], pp[:, k % 2, :], ACT.Tanh, scale=GELU_C * GELU_A) \
                        .then_inc(tanh_ready, 1)

                def centred_square(t):
                    act.wait_ge(centred, l * 4 + (t + 1))
                    if t >= 2:
                        act.wait_ge(gvar_ready, l * 4 + (t - 1))
                    act.activation(sq[:, t % 2, :], gv[:, t, :], ACT.Square).then_inc(csq_ready, 1)

                def pt_evict(c):
                    for f in range(2 * c, 2 * c + 2):
                        act.wait_ge(pt_filled, l * 8 + (f + 1))
                        act.copy(band[:, c, 4 * (f % 2):4 * (f % 2) + 4, :],
                                 bank[4 + f % 4][:, :].rearrange("p (n k) -> p n k", n=4)).then_inc(pt_taken, 1)

                high(l, 3)
                std(2 * l, True)
                for pos in range(1, GV_POS + 1):
                    high(l, pos + 3)
                for c in range(3):
                    high(l, GV_POS + c + 4)
                    softmax(c)
                for nh in range(2):
                    act.wait_ge(vband_filled, l * 2 + (nh + 1))
                    act.copy(vband[:, 4 * nh:4 * nh + 4, :],
                             bank[2 + nh][:, :].rearrange("p (n k) -> p n k", n=4)).then_inc(vband_taken, 1)
                act.wait_ge(r_ready, l * 3 + 2)
                for t in range(NTOK):
                    if t < NTOK - 1:
                        act.wait_ge(gv_done, l * 3 + (t + 1))
                    else:
                        act.wait_ge(group_done, group_value(l, GV_POS + 3))
                    if t >= 2:
                        act.wait_ge(gelu_ready, l * 8 + (t - 1))
                    act.mul(z[:, t % 2, :], bank[4 + t][:, :], rcol[:, t:t + 1])
                    act.activation(pp[:, t % 2, :], bank[4 + t][:, :], ACT.Square, scale=rcol[:, t:t + 1]) \
                        .then_inc(square_ready, 1)
                    if t >= 1:
                        tanh(t - 1)
                    if t >= 2:
                        centred_square(t - 2)
                    if t == 1:
                        softmax(3)
                high(l, U_POS + 3)
                tanh(3)
                centred_square(2)
                centred_square(3)
                act.wait_ge(gvar_ready, l * 4 + 4)
                act.activation(grstd[:, :, :], gvar[:, :, :], ACT.Sqrt, scale=1.0 / HD, bias=eps[:, 1:2]) \
                    .then_inc(gstd_ready, 1)
                for c in range(4):
                    high(l, U_POS + c + 4)
                    pt_evict(c)
                    act.wait_ge(evicted, evicted_value(l, 6 + c))
                    act.wait_ge(gelu_ready, l * 8 + (c + 3))
                    act.activation(pp[:, c % 2, :], z[:, c % 2, :], ACT.Square).then_inc(square_ready, 1)
                    tanh(4 + c)
                for b in range(4):
                    act.wait_ge(pv_filled, l * 4 + (b + 1))
                    act.copy(ahi[:, 0:4, b * P:(b + 1) * P].rearrange("p t (n q) -> p t n q", n=2),
                             bank[4 + b][:, :].rearrange("p (n t q) -> p t n q", n=2, t=4)).then_inc(att_hi, 1)
                for pr in range(4):
                    act.wait_ge(sgu_ready, l * 4 + (pr + 1))
                    act.copy(ahi[:, 4 + pr, :], pp[:, pr % 2, :]).then_inc(sgu_hi, 1)

                for m in range(KC):
                    high(l, WO_POS + m + 4)
                    act.wait_ge(evicted, evicted_value(l, fm_of(WO_POS + m)))
                    norm_chunk(2 * l + 1, m, gain[:, bass.ds(l * (2 * KC) + (KC + m), 1)])
                std(2 * l + 1, False)

                def quarter(q, last):
                    for m in range(KC):
                        high(l, MLP_POS + m + 4, q)
                        act.wait_ge(hid_ready, l * (QUARTERS * KC) + q * KC + (m + 1))
                        act.copy(ahi[:, m, :], pp[:, m % 2, :]).then_inc(hid_hi, 1)
                    for m in range(KC):
                        if not last or m < KC - 4:
                            high(l, MLP_POS + KC + m + 4, q)
                        if last:
                            act.wait_ge(evicted, l * FM_PER_LAYER + q * PER_QUARTER
                                        + (fm_of(MLP_POS + KC + m) + 1 + CREDIT))
                            norm_chunk(2 * l + 2, m, gain[:, bass.ds(l * (2 * KC) + (2 * KC + m), 1)])

                with act.Fori(0, QUARTERS - 1) as q:
                    quarter(q, False)
                quarter(QUARTERS - 1, True)
            std(2 * DEPTH, False)

        @block.vector
        def _(dve):
            def norm_low(norm, m, gain_col):
                dve.wait_ge(xhi_ready, norm * KC + (m + 1))
                dve.scalar_tensor_tensor(xlo[:, m, :], xt[:, m, :], gain_col, xhi[:, m, :],
                                         ALU.mult, ALU.subtract).then_inc(xlo_ready, 1)
                if m >= 1:
                    dve.wait_ge(sq_ready, norm * KC + (m + 1))
                    if m >= 2:
                        dve.wait_ge(sumsq_steps, norm * (KC - 1) + (m - 1))
                    dve.tensor_tensor(sumsq[:, :], sumsq[:, :], sq[:, m % 2, :], ALU.add).then_inc(sumsq_steps, 1)

            def rms(norm, columns):
                dve.wait_ge(std_ready, norm + 1)
                dve.reciprocal(rbc[:, :], rbc[:, :]).then_inc(r_ready, 1)
                if columns:
                    dve.reciprocal(rcol[:, :], rcol[:, :]).then_inc(r_ready, 1)

            dve.memset(ones[:, :], 1.0).then_inc(zeros_set, 1)
            dve.memset(kt[:, 0:CHUNK], 0.0).then_inc(zeros_set, 1)
            dve.memset(vt[:, 0:CHUNK], 0.0).then_inc(group_done, CREDIT)
            dve.memset(sinkarg[:, :, :], 0.0).then_inc(evicted, CREDIT)
            dve.wait_ge(gain_landed, 16)
            for m in range(KC):
                dve.wait_ge(x_landed[m], 16)
                norm_low(0, m, gain[:, m:m + 1])
            dve.wait_ge(const_landed, 16 * 4)

            with dve.Fori(0, DEPTH) as l:
                def scaled(pos, dst):
                    dve.wait_ge(group_done, group_value(l, pos))
                    by_chunk = lambda ap: ap.rearrange("p (n q) -> p n q", n=NCH)
                    dve.tensor_tensor(dst, by_chunk(bank[fm_of(pos) % BANKS][:, :]), by_chunk(rbc[:, :]),
                                      ALU.mult).then_inc(evicted, 1)

                def scores(c):
                    for f in range(2 * c, 2 * c + 2):
                        dve.wait_ge(scores_filled, l * 8 + (f + 1))
                        src = bank[(2 + f) % BANKS]
                        first = 1 if f % 2 == 0 else 0
                        if first:
                            dve.scalar_tensor_tensor(band[:, c, 0, :], src[:, 0:P], HD ** -0.5, bias[:, c, 1, :],
                                                     ALU.mult, ALU.add)
                        n0 = 4 * (f % 2)
                        dve.scalar_tensor_tensor(
                            band[:, c, n0 + first:n0 + 4, :],
                            src[:, first * P:].rearrange("p (n k) -> p n k", k=P), HD ** -0.5,
                            bias[:, c, 0:1, :].broadcast_to([P, 4 - first, P]), ALU.mult, ALU.add).then_inc(scores_taken, 1)
                    dve.wait_ge(scores_taken, l * 8 + (2 * c + 2))
                    dve.tensor_reduce(rowmax[:, c, :], band[:, c, :, :], AX.X, ALU.max).then_inc(rowmax_ready, 1)
                    dve.wait_ge(rowmax_ready, l * 4 + (c + 1))
                    s_col = sink_now[:, c:c + 1]
                    dve.tensor_scalar(negmax[:, c, :], rowmax[:, c, :], s_col, -1.0, ALU.max, ALU.mult) \
                        .then_inc(negmax_ready, 1)
                    dve.wait_ge(negmax_ready, l * 4 + (c + 1))
                    dve.tensor_scalar(sinkarg[:, c, :], negmax[:, c, :], s_col, None, ALU.add).then_inc(sinkarg_ready, 1)

                def normalise(c):
                    dve.wait_ge(exps_done, l * 4 + (c + 1))
                    dve.tensor_tensor(dsum[:, c, :], den[:, c, :], sinkexp[:, c, :], ALU.add).then_inc(dsum_ready, 1)
                    dve.wait_ge(dsum_ready, l * 4 + (c + 1))
                    dve.reciprocal(rden[:, c, :], dsum[:, c, :]).then_inc(rden_ready, 1)
                    dve.wait_ge(rden_ready, l * 4 + (c + 1))
                    dve.tensor_tensor(band[:, c, :, :], band[:, c, :, :],
                                      rden[:, c, :].rearrange("p (n a) -> p n a", a=1).broadcast_to([P, NCH, P]), ALU.mult) \
                        .then_inc(probs_ready, 1)

                def poly(k):
                    dve.wait_ge(square_ready, l * 8 + (k + 1))
                    dve.scalar_tensor_tensor(pp[:, k % 2, :], pp[:, k % 2, :], 1.0 / GELU_A, z[:, k % 2, :],
                                             ALU.add, ALU.mult).then_inc(poly_ready, 1)

                def gate(k, dst):
                    dve.wait_ge(tanh_ready, l * 8 + (k + 1))
                    dve.scalar_tensor_tensor(dst, pp[:, k % 2, :], 1.0, z[:, k % 2, :],
                                             ALU.add, ALU.mult).then_inc(gelu_ready, 1)

                def by_group(ap):
                    return ap.rearrange("p (g c) -> p g c", g=GROUPS)

                def centre(t):
                    dve.wait_ge(gelu_ready, l * 8 + (t + 1))
                    dve.tensor_reduce(gsum[:, t, :], by_group(gv[:, t, :]), AX.X, ALU.add).then_inc(gsum_ready, 1)
                    dve.wait_ge(gsum_ready, l * 4 + (t + 1))
                    dve.scalar_tensor_tensor(
                        by_group(gv[:, t, :]), gsum[:, t, :].rearrange("p (g a) -> p g a", a=1).broadcast_to([P, GROUPS, HD]),
                        -1.0 / HD, by_group(gv[:, t, :]), ALU.mult, ALU.add).then_inc(centred, 1)

                def variance(t):
                    dve.wait_ge(csq_ready, l * 4 + (t + 1))
                    dve.tensor_reduce(gvar[:, t, :], by_group(sq[:, t % 2, :]), AX.X, ALU.add).then_inc(gvar_ready, 1)

                dve.tensor_copy(sink_now[:, :], sink[:, bass.ds(l * 4, 4)]).then_inc(sink_taken, 1)
                rms(2 * l, True)
                dve.wait_ge(sink_taken, l + 1)
                dve.wait_ge(r_ready, l * 3 + 1)
                scaled(K_POS, kt[:, CHUNK:].rearrange("p (n q) -> p n q", n=NCH))
                scaled(V_POS, vt[:, CHUNK:].rearrange("p (n q) -> p n q", n=NCH))
                for t in range(4):
                    scaled(Q_POS + t, qt[:, :, t, :])
                scores(0)
                scores(1)
                normalise(0)
                scores(2)
                normalise(1)
                scores(3)
                poly(0)
                normalise(2)
                for t in range(NTOK):
                    if t >= 1:
                        poly(t)
                    gate(t, gv[:, t, :])
                    centre(t)
                    if t >= 1:
                        variance(t - 1)
                    if t == 1:
                        normalise(3)
                variance(NTOK - 1)
                dve.wait_ge(gstd_ready, l + 1)
                dve.reciprocal(grstd[:, :, :], grstd[:, :, :]).then_inc(grstd_ready, 1)
                dve.wait_ge(grstd_ready, l + 1)
                for t in range(NTOK):
                    dve.tensor_tensor(by_group(gv[:, t, :]), by_group(gv[:, t, :]),
                                      grstd[:, t, :].rearrange("p (g a) -> p g a", a=1).broadcast_to([P, GROUPS, HD]),
                                      ALU.mult).then_inc(vn_ready, 1)
                for c in range(4):
                    scaled(U_POS + c, z[:, c % 2, :].rearrange("p (n q) -> p n q", n=NCH))
                    poly(4 + c)
                    gate(4 + c, ut[:, c, :])
                for b in range(4):
                    dve.wait_ge(att_hi, l * 4 + (b + 1))
                    a = slice(b * P, (b + 1) * P)
                    dve.tensor_tensor(alo[:, 0:4, a].rearrange("p t (n q) -> p t n q", n=2),
                                      bank[4 + b][:, :].rearrange("p (n t q) -> p t n q", n=2, t=4),
                                      ahi[:, 0:4, a].rearrange("p t (n q) -> p t n q", n=2),
                                      ALU.subtract).then_inc(att_lo, 1)
                dve.wait_ge(gelu_ready, l * 8 + 8)

                def sgu_low(pr):
                    dve.wait_ge(sgu_hi, l * 4 + (pr + 1))
                    dve.tensor_tensor(alo[:, 4 + pr, :], pp[:, pr % 2, :], ahi[:, 4 + pr, :], ALU.subtract) \
                        .then_inc(sgu_lo, 1)

                for pr in range(4):
                    dve.wait_ge(sgu_filled, l * 4 + (pr + 1))
                    dve.tensor_tensor(z[:, pr % 2, :].rearrange("p (t i) -> p t i", t=NTOK),
                                      bank[(10 + pr) % BANKS][:, :].rearrange("p (t i) -> p t i", t=NTOK),
                                      bsb[:, pr:pr + 1, :].broadcast_to([P, NTOK, P]), ALU.add).then_inc(sgu_taken, 1)
                    if pr >= 1:
                        sgu_low(pr - 1)
                    dve.wait_ge(sgu_taken, l * 4 + (pr + 1))
                    dve.scalar_tensor_tensor(pp[:, pr % 2, :], z[:, pr % 2, :], 0.5, ut[:, pr, :],
                                             ALU.mult, ALU.mult).then_inc(sgu_ready, 1)
                sgu_low(3)

                def residual(q, pos, m):
                    dve.wait_ge(group_done, l * PER_LAYER + q * PER_QUARTER + (pos + 1 + CREDIT))
                    dve.tensor_tensor(xt[:, m, :], bank[fm_of(pos) % BANKS][:, :], xt[:, m, :], ALU.add) \
                        .then_inc(evicted, 1)

                for m in range(KC):
                    residual(0, WO_POS + m, m)
                    if m >= 1:
                        norm_low(2 * l + 1, m - 1, gain[:, bass.ds(l * (2 * KC) + (KC + m - 1), 1)])
                norm_low(2 * l + 1, KC - 1, gain[:, bass.ds(l * (2 * KC) + (2 * KC - 1), 1)])
                rms(2 * l + 1, False)

                def quarter(q, last):
                    def hidden_low(m):
                        dve.wait_ge(hid_hi, l * (QUARTERS * KC) + q * KC + (m + 1))
                        dve.tensor_tensor(alo[:, m, :], pp[:, m % 2, :], ahi[:, m, :], ALU.subtract) \
                            .then_inc(hid_lo, 1)

                    dve.wait_ge(r_ready, l * 3 + 3)
                    for m in range(KC):
                        pos = MLP_POS + m
                        dve.wait_ge(group_done, l * PER_LAYER + q * PER_QUARTER + (pos + 1 + CREDIT))
                        dve.tensor_tensor(z[:, m % 2, :], bank[fm_of(pos) % BANKS][:, :], rbc[:, :], ALU.mult) \
                            .then_inc(evicted, 1)
                        if m >= 1:
                            hidden_low(m - 1)
                        dve.wait_ge(evicted, l * FM_PER_LAYER + q * PER_QUARTER + (fm_of(pos) + 1 + CREDIT))
                        dve.scalar_tensor_tensor(pp[:, m % 2, :], z[:, m % 2, :], 0.0, z[:, m % 2, :],
                                                 ALU.max, ALU.mult).then_inc(hid_ready, 1)
                    hidden_low(KC - 1)
                    for m in range(KC):
                        residual(q, MLP_POS + KC + m, m)
                        if last and m >= 1:
                            norm_low(2 * l + 2, m - 1, gain[:, bass.ds(l * (2 * KC) + (2 * KC + m - 1), 1)])
                    if last:
                        norm_low(2 * l + 2, KC - 1, gain[:, bass.ds(l * (2 * KC) + (3 * KC - 1), 1)])

                with dve.Fori(0, QUARTERS - 1) as q:
                    quarter(q, False)
                quarter(QUARTERS - 1, True)

            rms(2 * DEPTH, False)
            dve.wait_ge(r_ready, 3 * DEPTH + 1)
            for m in range(KC):
                g = gain[:, 2 * DEPTH * KC + m:2 * DEPTH * KC + m + 1]
                dve.scalar_tensor_tensor(band[:, m // 2, (m % 2) * 4:(m % 2) * 4 + 4, :].rearrange("p n k -> p (n k)"),
                                         xt[:, m, :], g, rbc[:, :], ALU.mult, ALU.mult).then_inc(out_ready, 1)


def kernel(**inputs):
    import numpy as np
    import concourse.bacc as bacc
    from concourse.bass_utils import run_bass_kernel_spmd as run

    a = {k: np.asarray(v) for k, v in inputs.items()}
    L = DEPTH
    qw, kvw, sw = HQ * HD, 2 * HD, GROUPS * HD
    rows = lambda w: w.reshape(L, KC, P, -1)
    tiles = lambda w: rows(w).reshape(L, KC, P, -1, P).transpose(0, 3, 2, 1, 4).reshape(L, -1, P, D)
    w_in = a["w_in"]
    q_cols = w_in[:, :, :qw].reshape(L, D, 2, 4, HD).transpose(0, 1, 3, 2, 4).reshape(L, D, qw)
    at = [qw, qw + kvw, qw + 2 * kvw, qw + 2 * kvw + sw, qw + 2 * kvw + 2 * sw]
    k_cols, v_cols, u_cols, gv_cols = (w_in[:, :, s:e] for s, e in zip(at, at[1:]))
    gv_part = rows(gv_cols).reshape(L, 4, 2, P, sw).transpose(0, 1, 3, 2, 4).reshape(L, 4, P, D)
    w_o = a["w_o"]
    att_rows = w_o[:, :qw].reshape(L, 2, 4, HD, D).transpose(0, 2, 1, 3, 4).reshape(L, qw, D)
    wo = np.concatenate([att_rows, w_o[:, qw:]], axis=1)
    up = tiles(a["w_up"]).reshape(L, QUARTERS, KC, P, D)
    down = a["w_down"].reshape(L, QUARTERS, KC, P, KC, P).transpose(0, 1, 4, 3, 2, 5).reshape(L, QUARTERS, KC, P, D)
    mlp = np.concatenate([up, down], axis=2).reshape(L, -1, P, D)
    stream = np.concatenate([tiles(k_cols), tiles(v_cols), tiles(q_cols), gv_part, tiles(u_cols), tiles(wo), mlp],
                            axis=1).reshape(L * PER_LAYER, P, D)
    norms = np.stack([a["norm_mix"][0], a["norm_ffn"][0], a["norm_mix"][1], a["norm_ffn"][1], a["norm_final"]])
    dist = np.abs(np.arange(CHUNK)[:, None] + CHUNK - np.arange(P)[None, :])
    alibi = np.zeros((2, CHUNK, 4, 2, P), np.float32)
    for c in range(4):
        for r in range(2):
            head = 4 * (c // 2) + 2 * (c % 2) + r
            alibi[r, :, c, 0] = alibi[r, :, c, 1] = -(2.0 ** (-8.0 * (head + 1) / HQ)) * dist
    alibi[:, :, :, 1, :CHUNK] = LOWEST
    arrays = {
        "x_in": a["x"][0].T.reshape(KC, P, SEQ),
        "gains_in": norms.reshape(5, KC, P).transpose(2, 0, 1).reshape(P, 5 * KC),
        "weights_in": stream,
        "sinks_in": a["sinks"].reshape(L, 4, 2).transpose(2, 0, 1),
        "ws_in": a["w_s"].transpose(0, 3, 1, 2),
        "bs_in": a["b_s"].reshape(L, 4, 2, P).transpose(2, 0, 1, 3),
        "alibi_in": alibi.reshape(P, 8 * P),
        "ident_in": np.eye(P, dtype=np.float32),
    }
    arrays = {k: np.ascontiguousarray(v) for k, v in arrays.items()}
    nc = bacc.Bacc("TRN2", target_bir_lowering=False, num_devices=1)
    ap = {k: nc.dram_tensor(k, v.shape, mybir.dt.from_np(v.dtype), kind="ExternalInput").ap()
          for k, v in arrays.items()}
    out = nc.dram_tensor("out_t", (KC, P, SEQ), F32, kind="ExternalOutput").ap()
    build(nc, ap["x_in"], ap["gains_in"], ap["weights_in"], ap["sinks_in"].rearrange("r l c -> l r c"), ap["ws_in"],
          ap["bs_in"].rearrange("r l c i -> l r c i"), ap["alibi_in"], ap["ident_in"], out)
    r = run(nc, [arrays], core_ids=[0])
    return np.ascontiguousarray(r.results[0]["out_t"].reshape(D, SEQ).T).reshape(1, SEQ, D)
```

```python
from contextlib import ExitStack

import concourse.bass as bass
from concourse import mybir

F32 = mybir.dt.float32
F32R = mybir.dt.float32r
ALU = mybir.AluOpType
ACT = mybir.ActivationFunctionType
AX = mybir.AxisListType

P = 128
DEPTH = 2
SEQ = 512
D = 1024
KC = D // P
CHUNK = 64
NCH = SEQ // CHUNK
HD = 64
HQ = 8
NTOK = SEQ // P
GROUPS = 8
FF = 4 * D
QUARTERS = FF // D
EPS = 1e-6
GELU_C = 0.7978845608028654
GELU_A = 0.044715
LOWEST = -3.4028234663852886e38

GV_POS, K_POS, Q_POS, V_POS, U_POS, WO_POS, MLP_POS = 0, 4, 5, 9, 10, 14, 22
PER_QUARTER = 2 * KC
PER_LAYER = MLP_POS + QUARTERS * PER_QUARTER
SLOTS = 4
BANKS = 4
CREDIT = 4
OUT_BY_DVE = 5
WARM = 4
BY_POOL = 3


def slot_of(pos):
    return (pos - MLP_POS) % SLOTS


SLOT_USES = [sum(slot_of(i) == s for i in range(PER_LAYER)) for s in range(SLOTS)]


def landed_value(layer, pos):
    s = slot_of(pos)
    before = sum(slot_of(i) == s for i in range(pos))
    return (layer * SLOT_USES[s] + before + 1) * 16


def mlp_landed_value(layer, quad, s):
    before = sum(slot_of(i) == s for i in range(MLP_POS))
    return (layer * SLOT_USES[s] + before + quad + 1) * 16


def before_in_slot(pos):
    s = slot_of(pos)
    back = [i for i in range(pos) if slot_of(i) == s]
    return back[-1] if back else max(i for i in range(PER_LAYER) if slot_of(i) == s) - PER_LAYER


FM_PER_LAYER = PER_LAYER - K_POS


def fm_of(pos):
    return pos - K_POS


def bank_of(fm):
    return (fm + 2) % BANKS


def before_in_bank(fm):
    if fm >= BANKS:
        return fm - BANKS
    return max(j for j in range(FM_PER_LAYER) if bank_of(j) == bank_of(fm)) - FM_PER_LAYER


C_ORDER = (0, 2, 1, 3)


def build(nc, x, gains, weights, sinks, ws, bs, alibi, ident_in, out):
    with ExitStack() as ctx:
        def sb(name, shape, dt=F32):
            return ctx.enter_context(nc.sbuf_tensor(name, shape, dt))

        def sem(name):
            return ctx.enter_context(nc.semaphore(name))

        raw = sb("raw", [P, SLOTS, D])
        whi = sb("whi", [P, SLOTS, D], F32R)
        wlo = sb("wlo", [P, SLOTS, D], F32R)
        xt = sb("xt", [P, KC, SEQ])
        xhi = sb("xhi", [P, KC, SEQ], F32R)
        xlo = sb("xlo", [P, KC, SEQ], F32R)
        ahi = sb("ahi", [P, KC, SEQ], F32R)
        alo = sb("alo", [P, KC, SEQ], F32R)
        sumsq = sb("sumsq", [P, SEQ])
        sq = sb("sq", [P, 2, SEQ])
        rbc = sb("rbc", [P, SEQ])
        diag = sb("diag", [P, NTOK, P])
        rcol = sb("rcol", [P, NTOK])
        kt = sb("kt", [P, CHUNK + SEQ])
        vt = sb("vt", [P, CHUNK + SEQ])
        qt = sb("qt", [P, NCH, 4, CHUNK])
        vband = sb("vband", [P, NCH, P])
        band = sb("band", [P, 4, NCH, P])
        negmax = sb("negmax", [P, 4, NCH])
        rowmax = sb("rowmax", [P, 4, NCH])
        sinkarg = sb("sinkarg", [P, 4, NCH])
        sinkexp = sb("sinkexp", [P, 4, NCH])
        den = sb("den", [P, 4, NCH])
        dsum = sb("dsum", [P, 4, NCH])
        rden = sb("rden", [P, 4, NCH])
        ut = sb("ut", [P, 4, SEQ])
        gv = sb("gv", [P, NTOK, SEQ])
        z = sb("z", [P, 2, SEQ])
        pp = sb("pp", [P, 2, SEQ])
        gsum = sb("gsum", [P, NTOK, GROUPS])
        gvar = sb("gvar", [P, NTOK, GROUPS])
        grstd = sb("grstd", [P, NTOK, GROUPS])
        wst = sb("wst", [P, GROUPS, P])
        bsb = sb("bsb", [P, 4, P])
        gain = sb("gain", [P, (2 * DEPTH + 1) * KC])
        sink = sb("sink", [P, DEPTH * 4])
        sink_now = sb("sink_now", [P, 4])
        bias = sb("bias", [P, 4, 2, P])
        ident = sb("ident", [P, P])
        ones = sb("ones", [P, P])
        eps = sb("eps", [P, 2])
        root = sb("root", [P, 1])
        zero = sb("zero", [P, 1])

        bank = [ctx.enter_context(nc.psum_tensor(f"bank{i}", [P, 512], F32)) for i in range(8)]

        raw_landed = [sem(f"raw_landed{s}") for s in range(SLOTS)]
        x_landed = [sem(f"x_landed{m}") for m in range(KC // 2)]
        gain_landed = sem("gain_landed")
        const_landed = sem("const_landed")
        gate_landed = sem("gate_landed")
        ones_set = sem("ones_set")
        zeros_set = sem("zeros_set")
        zero_set = sem("zero_set")
        whi_ready = sem("whi_ready")
        half_ready = sem("half_ready")
        diag_zeroed = sem("diag_zeroed")
        diag_ready = sem("diag_ready")
        r_filled = sem("r_filled")
        rbc_ready = sem("rbc_ready")
        whi_by_pool = sem("whi_by_pool")
        wlo_ready = sem("wlo_ready")
        group_done = sem("group_done")
        evicted = sem("evicted")
        xhi_ready = sem("xhi_ready")
        xlo_ready = sem("xlo_ready")
        sq_ready = sem("sq_ready")
        sumsq_steps = sem("sumsq_steps")
        stat_filled = sem("stat_filled")
        std_ready = sem("std_ready")
        rcol_ready = sem("rcol_ready")
        scores_filled = sem("scores_filled")
        scores_taken = sem("scores_taken")
        sink_taken = sem("sink_taken")
        rowmax_ready = sem("rowmax_ready")
        negmax_ready = sem("negmax_ready")
        sinkarg_ready = sem("sinkarg_ready")
        exps_done = sem("exps_done")
        dsum_ready = sem("dsum_ready")
        rden_ready = sem("rden_ready")
        probs_ready = sem("probs_ready")
        vband_filled = sem("vband_filled")
        vband_taken = sem("vband_taken")
        pt_filled = sem("pt_filled")
        pt_taken = sem("pt_taken")
        pv_filled = sem("pv_filled")
        att_hi = sem("att_hi")
        att_lo = sem("att_lo")
        gv_done = sem("gv_done")
        square_ready = sem("square_ready")
        poly_ready = sem("poly_ready")
        tanh_ready = sem("tanh_ready")
        gelu_ready = sem("gelu_ready")
        gsum_ready = sem("gsum_ready")
        centred = sem("centred")
        csq_ready = sem("csq_ready")
        gvar_ready = sem("gvar_ready")
        gstd_ready = sem("gstd_ready")
        grstd_ready = sem("grstd_ready")
        vn_ready = sem("vn_ready")
        sgu_filled = sem("sgu_filled")
        sgu_taken = sem("sgu_taken")
        sgu_ready = sem("sgu_ready")
        sgu_hi = sem("sgu_hi")
        sgu_lo = sem("sgu_lo")
        hid_ready = sem("hid_ready")
        hid_hi = sem("hid_hi")
        hid_lo = sem("hid_lo")
        out_ready = sem("out_ready")
        out_by_pool = sem("out_by_pool")
        scaled_ready = sem("scaled_ready")
        out_stored = sem("out_stored")

        def sgu_bank(pr):
            return 4 + (pr + 2) % 4

        def mixbuf(pr):
            return (vt if pr % 2 else kt)[:, CHUNK:]

        def group_value(layer, pos):
            return layer * PER_LAYER + (pos + 1 + CREDIT)

        def evicted_value(layer, fm):
            return layer * FM_PER_LAYER + (fm + 1 + CREDIT)

        def final(m):
            return band[:, m // 2, (m % 2) * 4:(m % 2) * 4 + 4, :].rearrange("p n k -> p (n k)")

        block = ctx.enter_context(nc.Block())

        @block.sync
        def _(sp):
            def load(layer, pos, group):
                sp.wait_ge(wlo_ready, group_value(layer, before_in_slot(pos)))
                sp.dma_start(raw[:, slot_of(pos), :], weights[bass.ds(group, 1)].rearrange("a p f -> (a p) f")) \
                    .then_inc(raw_landed[slot_of(pos)], 16)

            with sp.Fori(0, DEPTH) as l:
                for pos in range(MLP_POS):
                    load(l, pos, l * PER_LAYER + pos)
                    if pos == 3:
                        lo, hi = slice(0, CHUNK), slice(CHUNK, P)
                        wl = ws[bass.ds(l, 1)].rearrange("a j g i -> (a j) g i")
                        sp.dma_start(wst[lo, :, :], wl[lo, :, :]).then_inc(gate_landed, 16)
                        sp.dma_start(wst[hi, :, CHUNK:P], wl[hi, :, CHUNK:P]).then_inc(gate_landed, 16)
                        for r in range(2):
                            src = bs[bass.ds(l, 1), r].rearrange("a c i -> a (c i)").broadcast_to([HD, 4 * P])
                            sp.dma_start(bsb[r * HD:(r + 1) * HD, :, :].rearrange("p c i -> p (c i)"), src) \
                                .then_inc(gate_landed, 16)
                with sp.Fori(0, QUARTERS * PER_QUARTER // SLOTS) as quad:
                    for s in range(SLOTS):
                        sp.wait_ge(wlo_ready, l * PER_LAYER + quad * SLOTS + (MLP_POS + s - SLOTS + 1 + CREDIT))
                        group = l * PER_LAYER + quad * SLOTS + (MLP_POS + s)
                        sp.dma_start(raw[:, s, :], weights[bass.ds(group, 1)].rearrange("a p f -> (a p) f")) \
                            .then_inc(raw_landed[s], 16)
            for m in range(OUT_BY_DVE):
                sp.wait_ge(out_ready, m + 1)
                sp.dma_start(out[m], final(m)).then_inc(out_stored, 16)
            sp.wait_ge(out_stored, 16 * KC)

        @block.gpsimd
        def _(pool):
            pool.memset(zero[:, :], 0.0).then_inc(zero_set, 1)
            pool.memset(eps[:, 0:1], EPS)
            pool.memset(eps[:, 1:2], 4 * EPS).then_inc(wlo_ready, CREDIT)
            for m in range(2, KC, 2):
                pool.dma_start(xt[:, m:m + 2, :], x[m:m + 2].rearrange("m p t -> p m t")).then_inc(x_landed[m // 2], 16)
            pool.wait_ge(zero_set, 1)

            def low(slot, cols, ready):
                pool.tensor_tensor(wlo[:, slot, cols], raw[:, slot, cols], whi[:, slot, cols], ALU.subtract) \
                    .then_inc(ready, 1)

            with pool.Fori(0, DEPTH) as l:
                for pos in range(MLP_POS):
                    s = slot_of(pos)
                    if pos < BY_POOL:
                        pool.wait_ge(raw_landed[s], landed_value(l, pos))
                        pool.wait_ge(group_done, group_value(l, before_in_slot(pos)))
                        parts = 2 if pos == 0 else 1
                        for h in range(parts):
                            cols = slice(h * (D // parts), (h + 1) * (D // parts))
                            pool.tensor_tensor(whi[:, s, cols], raw[:, s, cols],
                                               zero[:, :].broadcast_to([P, D // parts]), ALU.add) \
                                .then_inc(whi_by_pool, 1)
                            pool.wait_ge(whi_by_pool, l * (BY_POOL + 1) + (pos + 1 + (h if pos == 0 else 1)))
                            if h < parts - 1:
                                low(s, cols, half_ready)
                        low(s, cols, wlo_ready)
                    else:
                        pool.wait_ge(whi_ready, l * (PER_LAYER - BY_POOL) + (pos - BY_POOL + 1))
                        low(s, slice(0, D), wlo_ready)
                with pool.Fori(0, QUARTERS * PER_QUARTER // SLOTS) as quad:
                    for s in range(SLOTS):
                        pool.wait_ge(whi_ready, l * (PER_LAYER - BY_POOL) + quad * SLOTS + (MLP_POS + s - BY_POOL + 1))
                        low(s, slice(0, D), wlo_ready)
            pool.wait_ge(rbc_ready, 2 * DEPTH + 1)
            for m in range(OUT_BY_DVE, KC):
                pool.wait_ge(scaled_ready, m - OUT_BY_DVE + 1)
                pool.tensor_tensor(final(m), gv[:, m - OUT_BY_DVE, :], rbc[:, :], ALU.mult).then_inc(out_by_pool, 1)

        @block.tensor
        def _(pe):
            def products(pos, lay, q, hi, lo, before_chunk=None, order=range(KC)):
                s = slot_of(pos)
                o = bank[bank_of(fm_of(pos))][:, :]
                pe.wait_ge(wlo_ready, lay * PER_LAYER + q * PER_QUARTER + (pos + 1 + CREDIT))
                for kc in order:
                    if before_chunk:
                        before_chunk(kc)
                    wc = slice(kc * P, (kc + 1) * P)
                    pe.matmul(o, wlo[:, s, wc], hi[:, kc, :], start=(kc == order[0]), stop=False)
                    pe.matmul(o, whi[:, s, wc], hi[:, kc, :], start=False, stop=False)
                    mm = pe.matmul(o, whi[:, s, wc], lo[:, kc, :], start=False, stop=(kc == order[-1]))
                mm.then_inc(group_done, 1)

            def statistics(norm, columns):
                pe.wait_ge(sumsq_steps, norm * (KC - 1) + (KC - 1))
                for t in range(NTOK):
                    mm = pe.matmul(columns[:, t:t + 1], sumsq[:, t * P:(t + 1) * P], ones[:, 0:1],
                                   start=True, stop=True)
                mm.then_inc(stat_filled, 1)

            def spread(norm, row):
                pe.wait_ge(diag_ready, norm + 1)
                for t in range(NTOK):
                    mm = pe.matmul(row[:, t * P:(t + 1) * P], ones[:, :], diag[:, t, :], start=True, stop=True)
                mm.then_inc(r_filled, 1)

            def bank_free(lay, fm):
                pe.wait_ge(evicted, evicted_value(lay, before_in_bank(fm)))

            pe.wait_ge(ones_set, 2)
            pe.wait_ge(diag_zeroed, 1)
            for i in range(WARM):
                pe.matmul(bank[7][:, :], ones[:, :], diag[:, :, :].rearrange("p t k -> p (t k)"),
                          start=True, stop=True)
            with pe.Fori(0, DEPTH) as l:
                for s4 in range(4):
                    pos = GV_POS + s4
                    s = slot_of(pos)
                    steps = [(t, b) for b in range(2) for t in range(NTOK)]
                    if s4 == 3:
                        steps.sort()
                    for t, b in steps:
                        tok = slice(t * P, (t + 1) * P)
                        kc, wc = 2 * s4 + b, slice(b * 512, (b + 1) * 512)
                        if s4 == 0 and b == 0 and t == 0:
                            pe.wait_ge(half_ready, l + 1)
                        elif t == 0 and (s4 == 0 or b == 0):
                            pe.wait_ge(wlo_ready, group_value(l, pos))
                        if t == 0:
                            pe.wait_ge(xlo_ready, l * (2 * KC) + (kc + 1))
                        o = bank[4 + t][:, :]
                        pe.matmul(o, xhi[:, kc, tok], wlo[:, s, wc], start=(kc == 0), stop=False)
                        pe.matmul(o, xhi[:, kc, tok], whi[:, s, wc], start=False, stop=False)
                        mm = pe.matmul(o, xlo[:, kc, tok], whi[:, s, wc], start=False, stop=(kc == KC - 1))
                        if s4 == 3 and b == 1 and t < NTOK - 1:
                            mm.then_inc(gv_done, 1)
                    mm.then_inc(group_done, 1)

                bank_free(l, 3)
                statistics(2 * l, bank[1])

                def project(pos):
                    fm = fm_of(pos)
                    if fm in (2, 3):
                        pe.wait_ge(rbc_ready, 2 * l + 1)
                    else:
                        bank_free(l, fm)
                    products(pos, l, 0, xhi, xlo)

                def scores(ci):
                    c = C_ORDER[ci]
                    half, tp = c // 2, c % 2
                    part = slice(half * HD, (half + 1) * HD)
                    pe.wait_ge(evicted, evicted_value(l, fm_of(Q_POS) + 2 * tp + 1))
                    for nh in range(2):
                        f = 2 * ci + nh
                        if f < 4:
                            pe.wait_ge(square_ready, l * 8 + (f + 1))
                        else:
                            pe.wait_ge(scores_taken, l * 8 + (f - 4 + 1))
                        for n in range(4 * nh, 4 * nh + 4):
                            mm = pe.matmul(bank[4 + f % 4][:, (n % 4) * P:(n % 4 + 1) * P],
                                           qt[part, n, 2 * tp:2 * tp + 2, :].rearrange("p t q -> p (t q)"),
                                           kt[part, n * CHUNK:n * CHUNK + P], start=True, stop=True)
                        mm.then_inc(scores_filled, 1)

                def turn_probs(ci):
                    c = C_ORDER[ci]
                    pe.wait_ge(probs_ready, l * 4 + (ci + 1))
                    for nh in range(2):
                        f = 2 * ci + nh
                        if ci == 0:
                            pe.wait_ge(scores_taken, l * 8 + (6 + nh + 1))
                        elif ci == 1:
                            pe.wait_ge(vband_taken, l * 2 + (nh + 1))
                        else:
                            pe.wait_ge(sgu_taken, l * 4 + (f - 4 + 1))
                        for n in range(4 * nh, 4 * nh + 4):
                            mm = pe.transpose(bank[4 + (f + 2) % 4][:, (n % 4) * P:(n % 4 + 1) * P],
                                              band[:, c, n, :], ident[:, :])
                        mm.then_inc(pt_filled, 1)

                project(K_POS)
                spread(2 * l, bank[0])
                project(Q_POS)
                project(Q_POS + 1)
                project(Q_POS + 2)
                scores(0)
                scores(1)
                project(Q_POS + 3)
                project(V_POS)
                scores(2)
                scores(3)
                project(U_POS)
                pe.wait_ge(const_landed, 16 * 4)
                pe.wait_ge(evicted, evicted_value(l, fm_of(V_POS)))
                for nh in range(2):
                    pe.wait_ge(scores_taken, l * 8 + (4 + nh + 1))
                    for n in range(4 * nh, 4 * nh + 4):
                        mm = pe.transpose(bank[4 + nh][:, (n % 4) * P:(n % 4 + 1) * P],
                                          vt[:, n * CHUNK:n * CHUNK + P], ident[:, :])
                    mm.then_inc(vband_filled, 1)
                project(U_POS + 1)
                turn_probs(0)
                turn_probs(1)
                project(U_POS + 2)

                def mix_positions(pr):
                    pe.wait_ge(pt_taken, l * 8 + (pr + 1))
                    for t in range(NTOK):
                        for r in range(2):
                            g = 2 * pr + r
                            mm = pe.matmul(bank[sgu_bank(pr)][r * HD:(r + 1) * HD, t * P:(t + 1) * P],
                                           gv[:, t, g * HD:(g + 1) * HD], wst[:, g, :], start=True, stop=True)
                    mm.then_inc(sgu_filled, 1)

                pe.wait_ge(gate_landed, l * 64 + 64)
                pe.wait_ge(zeros_set, 1)
                pe.wait_ge(vn_ready, l * 4 + 4)
                mix_positions(0)
                mix_positions(1)
                project(U_POS + 3)
                mix_positions(2)
                mix_positions(3)
                turn_probs(2)
                turn_probs(3)

                pe.wait_ge(pt_taken, l * 8 + 8)
                for b in range(4):
                    for n in range(2 * b, 2 * b + 2):
                        for half in range(2):
                            part = slice(half * HD, (half + 1) * HD)
                            mm = pe.matmul(bank[4 + b][part, (n % 2) * 256:(n % 2 + 1) * 256],
                                           vband[:, n, part], band[:, 2 * half:2 * half + 2, n, :],
                                           start=True, stop=True)
                    mm.then_inc(pv_filled, 1)

                def mixed(kc):
                    if kc == 0:
                        pe.wait_ge(att_lo, l * 4 + 4)
                    if kc >= 4:
                        pe.wait_ge(sgu_lo, l * 4 + (kc - 4 + 1))

                for m in range(KC):
                    pos = WO_POS + m
                    bank_free(l, fm_of(pos))
                    products(pos, l, 0, ahi, alo, mixed if m == 0 else None, order=(4, 5, 6, 7, 0, 1, 2, 3))

                def mlp_group(q, pos, hi, lo, before_chunk=None):
                    pe.wait_ge(evicted, l * FM_PER_LAYER + q * PER_QUARTER + (fm_of(pos) - BANKS + 1 + CREDIT))
                    products(pos, l, q, hi, lo, before_chunk)

                def rest_of_quarter(q):
                    for m in range(1, KC):
                        mlp_group(q, MLP_POS + m, xhi, xlo)
                    for m in range(KC):
                        mlp_group(q, MLP_POS + KC + m, ahi, alo,
                                  (lambda kc: pe.wait_ge(hid_lo, l * (QUARTERS * KC) + q * KC + (kc + 1)))
                                  if m == 0 else None)

                mlp_group(0, MLP_POS, xhi, xlo, lambda kc: pe.wait_ge(xlo_ready, l * (2 * KC) + (KC + kc + 1)))
                statistics(2 * l + 1, bank[4])
                spread(2 * l + 1, bank[5])
                with pe.Fori(0, QUARTERS - 1) as q:
                    rest_of_quarter(q)
                    mlp_group(q, MLP_POS + PER_QUARTER, xhi, xlo)
                rest_of_quarter(QUARTERS - 1)
            statistics(2 * DEPTH, bank[4])
            spread(2 * DEPTH, bank[5])

        @block.scalar
        def _(act):
            def high(l, pos, q=0):
                s = slot_of(pos)
                if pos < MLP_POS:
                    act.wait_ge(raw_landed[s], landed_value(l, pos))
                    act.wait_ge(group_done, group_value(l, before_in_slot(pos)))
                else:
                    k = pos - MLP_POS
                    act.wait_ge(raw_landed[s], l * (16 * SLOT_USES[s]) + q * (16 * PER_QUARTER // SLOTS)
                                + mlp_landed_value(0, k // SLOTS, s))
                    act.wait_ge(group_done, l * PER_LAYER + q * PER_QUARTER
                                + (pos - SLOTS + 1 + CREDIT))
                act.activation(whi[:, s, :], raw[:, s, :], ACT.Copy).then_inc(whi_ready, 1)

            def norm_chunk(norm, m, gain_col):
                act.mul(xhi[:, m, :], xt[:, m, :], gain_col).then_inc(xhi_ready, 1)
                dst = sumsq[:, :] if m == 0 else sq[:, m % 2, :]
                if m >= 3:
                    act.wait_ge(sumsq_steps, norm * (KC - 1) + (m - 2))
                act.activation(dst, xt[:, m, :], ACT.Square).then_inc(sq_ready, 1)

            def std(norm, columns):
                act.activation(root[:, :], eps[:, 0:1], ACT.Sqrt)
                act.wait_ge(stat_filled, norm + 1)
                act.activation(rcol[:, :], columns[:, 0:NTOK], ACT.Sqrt, scale=1.0 / D, bias=eps[:, 0:1]) \
                    .then_inc(std_ready, 1)

            def take_spread(norm, row):
                act.wait_ge(r_filled, norm + 1)
                act.copy(rbc[:, :], row[:, :]).then_inc(rbc_ready, 1)

            act.dma_start(gain[:, :], gains).then_inc(gain_landed, 16)
            act.dma_start(xt[:, 0:2, :], x[0:2].rearrange("m p t -> p m t")).then_inc(x_landed[0], 16)
            act.wait_ge(gain_landed, 16)
            act.wait_ge(wlo_ready, CREDIT)
            for m in range(KC):
                act.wait_ge(x_landed[m // 2], 16)
                norm_chunk(0, m, gain[:, m:m + 1])
            act.dma_start(ident[:, :], ident_in).then_inc(const_landed, 16)
            act.dma_start(bias[:, :, :, :].rearrange("p c a k -> p (c a k)"), alibi).then_inc(const_landed, 16)
            for r in range(2):
                src = sinks[:, r].rearrange("(a l) c -> a (l c)", a=1).broadcast_to([HD, DEPTH * 4])
                act.dma_start(sink[r * HD:(r + 1) * HD, :], src).then_inc(const_landed, 16)

            with act.Fori(0, DEPTH) as l:
                def softmax(ci):
                    c = C_ORDER[ci]
                    act.wait_ge(negmax_ready, l * 4 + (ci + 1))
                    for n in range(NCH):
                        act.activation(band[:, c, n, :], band[:, c, n, :], ACT.Exp, bias=negmax[:, c, n:n + 1],
                                       accum_out=den[:, c, n:n + 1])
                    act.wait_ge(sinkarg_ready, l * 4 + (ci + 1))
                    act.activation(sinkexp[:, c, :], sinkarg[:, c, :], ACT.Exp).then_inc(exps_done, 1)

                def square_gate(t):
                    if t < NTOK - 1:
                        act.wait_ge(gv_done, l * 3 + (t + 1))
                    else:
                        act.wait_ge(group_done, group_value(l, GV_POS + 3))
                    if t >= 2:
                        act.wait_ge(gelu_ready, l * 8 + (t - 1))
                    act.mul(z[:, t % 2, :], bank[4 + t][:, :], rcol[:, t:t + 1])
                    act.activation(pp[:, t % 2, :], bank[4 + t][:, :], ACT.Square, scale=rcol[:, t:t + 1]) \
                        .then_inc(square_ready, 1)

                def tanh(k):
                    act.wait_ge(poly_ready, l * 8 + (k + 1))
                    act.activation(pp[:, k % 2, :], pp[:, k % 2, :], ACT.Tanh, scale=GELU_C * GELU_A) \
                        .then_inc(tanh_ready, 1)

                def centred_square(t):
                    act.wait_ge(centred, l * 4 + (t + 1))
                    if t >= 2:
                        act.wait_ge(gvar_ready, l * 4 + (t - 1))
                    act.activation(sq[:, t % 2, :], gv[:, t, :], ACT.Square).then_inc(csq_ready, 1)

                def take_turned(ci):
                    c = C_ORDER[ci]
                    for f in range(2 * ci, 2 * ci + 2):
                        act.wait_ge(pt_filled, l * 8 + (f + 1))
                        act.copy(band[:, c, 4 * (f % 2):4 * (f % 2) + 4, :],
                                 bank[4 + (f + 2) % 4][:, :].rearrange("p (n k) -> p n k", n=4)).then_inc(pt_taken, 1)

                def product_high(pr):
                    act.wait_ge(sgu_ready, l * 4 + (pr + 1))
                    act.copy(ahi[:, 4 + pr, :], sq[:, pr % 2, :]).then_inc(sgu_hi, 1)

                def gelu_u(c):
                    act.wait_ge(evicted, evicted_value(l, fm_of(U_POS) + c))
                    act.wait_ge(gelu_ready, l * 8 + (c + 3))
                    act.activation(pp[:, c % 2, :], z[:, c % 2, :], ACT.Square).then_inc(square_ready, 1)
                    tanh(4 + c)

                for pos in range(3, 7):
                    high(l, pos)
                std(2 * l, bank[1])
                high(l, 7)
                act.wait_ge(rcol_ready, 2 * l + 1)
                square_gate(0)
                square_gate(1)
                tanh(0)
                take_spread(2 * l, bank[0])
                high(l, 8)
                square_gate(2)
                tanh(1)
                centred_square(0)
                high(l, 9)
                square_gate(3)
                tanh(2)
                centred_square(1)
                tanh(3)
                centred_square(2)
                high(l, 10)
                centred_square(3)
                act.wait_ge(gvar_ready, l * 4 + 4)
                act.activation(grstd[:, :, :], gvar[:, :, :], ACT.Sqrt, scale=1.0 / HD, bias=eps[:, 1:2]) \
                    .then_inc(gstd_ready, 1)
                high(l, 11)
                softmax(0)
                high(l, 12)
                softmax(1)
                high(l, 13)
                softmax(2)
                high(l, 14)
                for nh in range(2):
                    act.wait_ge(vband_filled, l * 2 + (nh + 1))
                    act.copy(vband[:, 4 * nh:4 * nh + 4, :],
                             bank[4 + nh][:, :].rearrange("p (n k) -> p n k", n=4)).then_inc(vband_taken, 1)
                gelu_u(0)
                softmax(3)
                high(l, 15)
                gelu_u(1)
                take_turned(0)
                take_turned(1)
                high(l, 16)
                gelu_u(2)
                for pr in range(2):
                    product_high(pr)
                high(l, 17)
                gelu_u(3)
                take_turned(2)
                take_turned(3)
                for pr in range(2, 4):
                    product_high(pr)
                for b in range(4):
                    act.wait_ge(pv_filled, l * 4 + (b + 1))
                    act.copy(ahi[:, 0:4, b * P:(b + 1) * P].rearrange("p t (n q) -> p t n q", n=2),
                             bank[4 + b][:, :].rearrange("p (n t q) -> p t n q", n=2, t=4)).then_inc(att_hi, 1)

                for m in range(KC):
                    act.wait_ge(evicted, evicted_value(l, fm_of(WO_POS + m)))
                    norm_chunk(2 * l + 1, m, gain[:, bass.ds(l * (2 * KC) + (KC + m), 1)])
                    high(l, WO_POS + m + 4)

                def hidden_high(q, m):
                    act.wait_ge(hid_ready, l * (QUARTERS * KC) + q * KC + (m + 1))
                    act.copy(ahi[:, m % KC, :], pp[:, m % 2, :]).then_inc(hid_hi, 1)
                    high(l, MLP_POS + m + 4, q)

                def rest_of_quarter(q, last):
                    for m in range(1, KC):
                        hidden_high(q, m)
                    for m in range(KC):
                        if last:
                            act.wait_ge(evicted, l * FM_PER_LAYER + q * PER_QUARTER
                                        + (fm_of(MLP_POS + KC + m) + 1 + CREDIT))
                            norm_chunk(2 * l + 2, m, gain[:, bass.ds(l * (2 * KC) + (2 * KC + m), 1)])
                        if not last or m < KC - 4:
                            high(l, MLP_POS + KC + m + 4, q)

                def next_first(q):
                    act.wait_ge(hid_ready, l * (QUARTERS * KC) + q * KC + (KC + 1))
                    act.copy(ahi[:, 0, :], pp[:, 0, :]).then_inc(hid_hi, 1)
                    high(l, MLP_POS + PER_QUARTER + 4, q)

                std(2 * l + 1, bank[4])
                take_spread(2 * l + 1, bank[5])
                hidden_high(0, 0)
                with act.Fori(0, QUARTERS - 1) as q:
                    rest_of_quarter(q, False)
                    next_first(q)
                rest_of_quarter(QUARTERS - 1, True)
            for m in range(OUT_BY_DVE, KC):
                g = gain[:, 2 * DEPTH * KC + m:2 * DEPTH * KC + m + 1]
                act.mul(gv[:, m - OUT_BY_DVE, :], xt[:, m, :], g).then_inc(scaled_ready, 1)
            std(2 * DEPTH, bank[4])
            take_spread(2 * DEPTH, bank[5])
            for m in range(OUT_BY_DVE, KC):
                act.wait_ge(out_by_pool, m - OUT_BY_DVE + 1)
                act.dma_start(out[m], final(m)).then_inc(out_stored, 16)

        @block.vector
        def _(dve):
            def norm_low(norm, m, gain_col):
                dve.wait_ge(xhi_ready, norm * KC + (m + 1))
                dve.scalar_tensor_tensor(xlo[:, m, :], xt[:, m, :], gain_col, xhi[:, m, :],
                                         ALU.mult, ALU.subtract).then_inc(xlo_ready, 1)

            def add_square(norm, m):
                if m >= 1:
                    dve.wait_ge(sq_ready, norm * KC + (m + 1))
                    if m >= 2:
                        dve.wait_ge(sumsq_steps, norm * (KC - 1) + (m - 1))
                    dve.tensor_tensor(sumsq[:, :], sumsq[:, :], sq[:, m % 2, :], ALU.add).then_inc(sumsq_steps, 1)

            def rms(norm):
                dve.wait_ge(std_ready, norm + 1)
                dve.reciprocal(rcol[:, :], rcol[:, :]).then_inc(rcol_ready, 1)
                dve.wait_ge(rcol_ready, norm + 1)
                dve.tensor_tensor(diag[:, :, :], ident[:, :].rearrange("p (a k) -> p a k", a=1).broadcast_to([P, NTOK, P]),
                                  rcol[:, :].rearrange("p (t a) -> p t a", a=1).broadcast_to([P, NTOK, P]),
                                  ALU.mult).then_inc(diag_ready, 1)

            dve.memset(wst[P // 2:P, :, 0:P // 2], 0.0).then_inc(zeros_set, 1)
            dve.memset(diag[:, :, :], 0.0).then_inc(diag_zeroed, 1)
            dve.memset(ones[:, :], 1.0).then_inc(ones_set, 1)
            dve.memset(kt[:, 0:CHUNK], 0.0).then_inc(ones_set, 1)
            dve.memset(vt[:, 0:CHUNK], 0.0).then_inc(group_done, CREDIT)
            dve.memset(sinkarg[:, :, :], 0.0).then_inc(evicted, CREDIT)
            dve.wait_ge(gain_landed, 16)
            for m in range(KC):
                dve.wait_ge(x_landed[m // 2], 16)
                norm_low(0, m, gain[:, m:m + 1])
                add_square(0, m)
            dve.wait_ge(const_landed, 16 * 4)

            with dve.Fori(0, DEPTH) as l:
                def scaled(pos, dst):
                    by_chunk = lambda ap: ap.rearrange("p (n q) -> p n q", n=NCH)
                    dve.wait_ge(group_done, group_value(l, pos))
                    dve.tensor_tensor(dst, by_chunk(bank[bank_of(fm_of(pos))][:, :]), by_chunk(rbc[:, :]),
                                      ALU.mult).then_inc(evicted, 1)

                def scores(ci):
                    c = C_ORDER[ci]
                    for f in range(2 * ci, 2 * ci + 2):
                        dve.wait_ge(scores_filled, l * 8 + (f + 1))
                        src = bank[4 + f % 4]
                        first = 1 if f % 2 == 0 else 0
                        if first:
                            dve.scalar_tensor_tensor(band[:, c, 0, :], src[:, 0:P], HD ** -0.5, bias[:, c, 1, :],
                                                     ALU.mult, ALU.add)
                        n0 = 4 * (f % 2)
                        dve.scalar_tensor_tensor(
                            band[:, c, n0 + first:n0 + 4, :],
                            src[:, first * P:].rearrange("p (n k) -> p n k", k=P), HD ** -0.5,
                            bias[:, c, 0:1, :].broadcast_to([P, 4 - first, P]), ALU.mult, ALU.add) \
                            .then_inc(scores_taken, 1)
                    dve.wait_ge(scores_taken, l * 8 + (2 * ci + 2))
                    dve.tensor_reduce(rowmax[:, c, :], band[:, c, :, :], AX.X, ALU.max).then_inc(rowmax_ready, 1)
                    dve.wait_ge(rowmax_ready, l * 4 + (ci + 1))
                    s_col = sink_now[:, c:c + 1]
                    dve.tensor_scalar(negmax[:, c, :], rowmax[:, c, :], s_col, -1.0, ALU.max, ALU.mult) \
                        .then_inc(negmax_ready, 1)
                    dve.wait_ge(negmax_ready, l * 4 + (ci + 1))
                    dve.tensor_scalar(sinkarg[:, c, :], negmax[:, c, :], s_col, None, ALU.add).then_inc(sinkarg_ready, 1)

                def normalise(ci):
                    c = C_ORDER[ci]
                    dve.wait_ge(exps_done, l * 4 + (ci + 1))
                    dve.tensor_tensor(dsum[:, c, :], den[:, c, :], sinkexp[:, c, :], ALU.add).then_inc(dsum_ready, 1)
                    dve.wait_ge(dsum_ready, l * 4 + (ci + 1))
                    dve.reciprocal(rden[:, c, :], dsum[:, c, :]).then_inc(rden_ready, 1)
                    dve.wait_ge(rden_ready, l * 4 + (ci + 1))
                    dve.tensor_tensor(band[:, c, :, :], band[:, c, :, :],
                                      rden[:, c, :].rearrange("p (n a) -> p n a", a=1).broadcast_to([P, NCH, P]),
                                      ALU.mult).then_inc(probs_ready, 1)

                def poly(k):
                    dve.wait_ge(square_ready, l * 8 + (k + 1))
                    dve.scalar_tensor_tensor(pp[:, k % 2, :], pp[:, k % 2, :], 1.0 / GELU_A, z[:, k % 2, :],
                                             ALU.add, ALU.mult).then_inc(poly_ready, 1)

                def gate(k, dst):
                    dve.wait_ge(tanh_ready, l * 8 + (k + 1))
                    dve.scalar_tensor_tensor(dst, pp[:, k % 2, :], 1.0, z[:, k % 2, :],
                                             ALU.add, ALU.mult).then_inc(gelu_ready, 1)

                def by_group(ap):
                    return ap.rearrange("p (g c) -> p g c", g=GROUPS)

                def centre(t):
                    dve.wait_ge(gelu_ready, l * 8 + (t + 1))
                    dve.tensor_reduce(gsum[:, t, :], by_group(gv[:, t, :]), AX.X, ALU.add).then_inc(gsum_ready, 1)
                    dve.wait_ge(gsum_ready, l * 4 + (t + 1))
                    dve.scalar_tensor_tensor(
                        by_group(gv[:, t, :]), gsum[:, t, :].rearrange("p (g a) -> p g a", a=1).broadcast_to([P, GROUPS, HD]),
                        -1.0 / HD, by_group(gv[:, t, :]), ALU.mult, ALU.add).then_inc(centred, 1)

                def variance(t):
                    dve.wait_ge(csq_ready, l * 4 + (t + 1))
                    dve.tensor_reduce(gvar[:, t, :], by_group(sq[:, t % 2, :]), AX.X, ALU.add).then_inc(gvar_ready, 1)

                def normed_gates():
                    dve.wait_ge(gstd_ready, l + 1)
                    dve.reciprocal(grstd[:, :, :], grstd[:, :, :]).then_inc(grstd_ready, 1)
                    dve.wait_ge(grstd_ready, l + 1)
                    for t in range(NTOK):
                        dve.tensor_tensor(by_group(gv[:, t, :]), by_group(gv[:, t, :]),
                                          grstd[:, t, :].rearrange("p (g a) -> p g a", a=1).broadcast_to([P, GROUPS, HD]),
                                          ALU.mult).then_inc(vn_ready, 1)

                def take(ap):
                    return ap.rearrange("p (n q) -> p n q", n=NCH)

                dve.tensor_copy(sink_now[:, :], sink[:, bass.ds(l * 4, 4)]).then_inc(sink_taken, 1)
                rms(2 * l)
                dve.wait_ge(sink_taken, l + 1)
                poly(0)
                poly(1)
                gate(0, gv[:, 0, :])
                centre(0)
                dve.wait_ge(rbc_ready, 2 * l + 1)
                scaled(K_POS, take(kt[:, CHUNK:]))
                poly(2)
                gate(1, gv[:, 1, :])
                variance(0)
                centre(1)
                scaled(Q_POS, qt[:, :, 0, :])
                poly(3)
                gate(2, gv[:, 2, :])
                variance(1)
                centre(2)
                gate(3, gv[:, 3, :])
                variance(2)
                centre(3)
                scaled(Q_POS + 1, qt[:, :, 1, :])
                variance(3)
                scaled(Q_POS + 2, qt[:, :, 2, :])
                normed_gates()
                scores(0)
                scores(1)
                scaled(Q_POS + 3, qt[:, :, 3, :])
                normalise(0)
                scaled(V_POS, take(vt[:, CHUNK:]))
                normalise(1)
                scores(2)
                scores(3)
                normalise(2)
                scaled(U_POS, take(z[:, 0, :]))
                poly(4)
                gate(4, ut[:, 0, :])
                normalise(3)
                scaled(U_POS + 1, take(z[:, 1, :]))
                poly(5)
                gate(5, ut[:, 1, :])
                scaled(U_POS + 2, take(z[:, 0, :]))
                poly(6)
                gate(6, ut[:, 2, :])

                def sgu_low(pr):
                    dve.wait_ge(sgu_hi, l * 4 + (pr + 1))
                    dve.tensor_tensor(alo[:, 4 + pr, :], sq[:, pr % 2, :], ahi[:, 4 + pr, :], ALU.subtract) \
                        .then_inc(sgu_lo, 1)

                def mixed(pr):
                    dve.wait_ge(sgu_filled, l * 4 + (pr + 1))
                    dve.tensor_tensor(mixbuf(pr).rearrange("p (t i) -> p t i", t=NTOK),
                                      bank[sgu_bank(pr)][:, :].rearrange("p (t i) -> p t i", t=NTOK),
                                      bsb[:, pr:pr + 1, :].broadcast_to([P, NTOK, P]), ALU.add).then_inc(sgu_taken, 1)

                def product(pr):
                    dve.wait_ge(gelu_ready, l * 8 + (4 + pr + 1))
                    dve.wait_ge(sgu_taken, l * 4 + (pr + 1))
                    dve.scalar_tensor_tensor(sq[:, pr % 2, :], mixbuf(pr), 0.5, ut[:, pr, :],
                                             ALU.mult, ALU.mult).then_inc(sgu_ready, 1)

                mixed(0)
                mixed(1)
                product(0)
                product(1)
                sgu_low(0)
                sgu_low(1)
                scaled(U_POS + 3, take(z[:, 1, :]))
                poly(7)
                mixed(2)
                mixed(3)
                gate(7, ut[:, 3, :])
                product(2)
                product(3)
                sgu_low(2)
                sgu_low(3)
                for b in range(4):
                    dve.wait_ge(att_hi, l * 4 + (b + 1))
                    a = slice(b * P, (b + 1) * P)
                    dve.tensor_tensor(alo[:, 0:4, a].rearrange("p t (n q) -> p t n q", n=2),
                                      bank[4 + b][:, :].rearrange("p (n t q) -> p t n q", n=2, t=4),
                                      ahi[:, 0:4, a].rearrange("p t (n q) -> p t n q", n=2),
                                      ALU.subtract).then_inc(att_lo, 1)

                def residual(q, pos, m):
                    dve.wait_ge(group_done, l * PER_LAYER + q * PER_QUARTER + (pos + 1 + CREDIT))
                    dve.tensor_tensor(xt[:, m, :], bank[bank_of(fm_of(pos))][:, :], xt[:, m, :], ALU.add) \
                        .then_inc(evicted, 1)

                def ffn_low(m):
                    norm_low(2 * l + 1, m, gain[:, bass.ds(l * (2 * KC) + (KC + m), 1)])

                def next_norm(m):
                    add_square(2 * l + 2, m)
                    norm_low(2 * l + 2, m, gain[:, bass.ds(l * (2 * KC) + (2 * KC + m), 1)])

                for m in range(KC):
                    residual(0, WO_POS + m, m)
                    if m >= 1:
                        ffn_low(m - 1)
                    if 1 <= m < KC - 1:
                        add_square(2 * l + 1, m - 1)
                ffn_low(KC - 1)
                add_square(2 * l + 1, KC - 2)
                add_square(2 * l + 1, KC - 1)

                def hidden_low(q, m):
                    dve.wait_ge(hid_hi, l * (QUARTERS * KC) + q * KC + (m + 1))
                    dve.tensor_tensor(alo[:, m % KC, :], pp[:, m % 2, :], ahi[:, m % KC, :], ALU.subtract) \
                        .then_inc(hid_lo, 1)

                def hidden(q, m, low_before=None):
                    pos = MLP_POS + m if m < KC else MLP_POS + PER_QUARTER
                    dve.wait_ge(group_done, l * PER_LAYER + q * PER_QUARTER + (pos + 1 + CREDIT))
                    dve.tensor_tensor(z[:, m % 2, :], bank[bank_of(fm_of(pos))][:, :], rbc[:, :], ALU.mult) \
                        .then_inc(evicted, 1)
                    if low_before is not None:
                        hidden_low(q, low_before)
                    dve.wait_ge(evicted, l * FM_PER_LAYER + q * PER_QUARTER + (fm_of(pos) + 1 + CREDIT))
                    dve.scalar_tensor_tensor(pp[:, m % 2, :], z[:, m % 2, :], 0.0, z[:, m % 2, :],
                                             ALU.max, ALU.mult).then_inc(hid_ready, 1)

                def rest_of_quarter(q, last):
                    for m in range(1, KC):
                        hidden(q, m, m - 1)
                    hidden_low(q, KC - 1)
                    for m in range(KC):
                        residual(q, MLP_POS + KC + m, m)
                        if last and m >= 1:
                            next_norm(m - 1)
                    if last:
                        next_norm(KC - 1)

                rms(2 * l + 1)
                dve.wait_ge(rbc_ready, 2 * l + 2)
                hidden(0, 0)
                with dve.Fori(0, QUARTERS - 1) as q:
                    rest_of_quarter(q, False)
                    hidden(q, KC)
                rest_of_quarter(QUARTERS - 1, True)

            rms(2 * DEPTH)
            dve.wait_ge(rbc_ready, 2 * DEPTH + 1)
            for m in range(OUT_BY_DVE):
                g = gain[:, 2 * DEPTH * KC + m:2 * DEPTH * KC + m + 1]
                dve.scalar_tensor_tensor(final(m), xt[:, m, :], g, rbc[:, :], ALU.mult, ALU.mult).then_inc(out_ready, 1)


def kernel(**inputs):
    import numpy as np
    import concourse.bacc as bacc
    from concourse.bass_utils import run_bass_kernel_spmd as run

    a = {k: np.asarray(v) for k, v in inputs.items()}
    L = DEPTH
    qw, kvw, sw = HQ * HD, 2 * HD, GROUPS * HD
    rows = lambda w: w.reshape(L, KC, P, -1)
    tiles = lambda w: rows(w).reshape(L, KC, P, -1, P).transpose(0, 3, 2, 1, 4).reshape(L, -1, P, D)
    w_in = a["w_in"]
    q_cols = w_in[:, :, :qw].reshape(L, D, 2, 4, HD).transpose(0, 1, 3, 2, 4).reshape(L, D, qw)
    at = [qw, qw + kvw, qw + 2 * kvw, qw + 2 * kvw + sw, qw + 2 * kvw + 2 * sw]
    k_cols, v_cols, u_cols, gv_cols = (w_in[:, :, s:e] for s, e in zip(at, at[1:]))
    gv_part = rows(gv_cols).reshape(L, 4, 2, P, sw).transpose(0, 1, 3, 2, 4).reshape(L, 4, P, D)
    w_o = a["w_o"]
    att_rows = w_o[:, :qw].reshape(L, 2, 4, HD, D).transpose(0, 2, 1, 3, 4).reshape(L, qw, D)
    wo = np.concatenate([att_rows, w_o[:, qw:]], axis=1)
    up = tiles(a["w_up"]).reshape(L, QUARTERS, KC, P, D)
    down = a["w_down"].reshape(L, QUARTERS, KC, P, KC, P).transpose(0, 1, 4, 3, 2, 5).reshape(L, QUARTERS, KC, P, D)
    mlp = np.concatenate([up, down], axis=2).reshape(L, -1, P, D)
    stream = np.concatenate([gv_part, tiles(k_cols), tiles(q_cols), tiles(v_cols), tiles(u_cols), tiles(wo), mlp],
                            axis=1).reshape(L * PER_LAYER, P, D)
    norms = np.stack([a["norm_mix"][0], a["norm_ffn"][0], a["norm_mix"][1], a["norm_ffn"][1], a["norm_final"]])
    dist = np.abs(np.arange(CHUNK)[:, None] + CHUNK - np.arange(P)[None, :])
    alibi = np.zeros((2, CHUNK, 4, 2, P), np.float32)
    for c in range(4):
        for r in range(2):
            head = 4 * (c // 2) + 2 * (c % 2) + r
            alibi[r, :, c, 0] = alibi[r, :, c, 1] = -(2.0 ** (-8.0 * (head + 1) / HQ)) * dist
    alibi[:, :, :, 1, :CHUNK] = LOWEST
    arrays = {
        "x_in": a["x"][0].T.reshape(KC, P, SEQ),
        "gains_in": norms.reshape(5, KC, P).transpose(2, 0, 1).reshape(P, 5 * KC),
        "weights_in": stream,
        "sinks_in": a["sinks"].reshape(L, 4, 2).transpose(2, 0, 1),
        "ws_in": a["w_s"].transpose(0, 3, 1, 2),
        "bs_in": a["b_s"].reshape(L, 4, 2, P).transpose(2, 0, 1, 3),
        "alibi_in": alibi.reshape(P, 8 * P),
        "ident_in": np.eye(P, dtype=np.float32),
    }
    arrays = {k: np.ascontiguousarray(v) for k, v in arrays.items()}
    nc = bacc.Bacc("TRN2", target_bir_lowering=False, num_devices=1)
    ap = {k: nc.dram_tensor(k, v.shape, mybir.dt.from_np(v.dtype), kind="ExternalInput").ap()
          for k, v in arrays.items()}
    out = nc.dram_tensor("out_t", (KC, P, SEQ), F32, kind="ExternalOutput").ap()
    build(nc, ap["x_in"], ap["gains_in"], ap["weights_in"], ap["sinks_in"].rearrange("r l c -> l r c"), ap["ws_in"],
          ap["bs_in"].rearrange("r l c i -> l r c i"), ap["alibi_in"], ap["ident_in"], out)
    r = run(nc, [arrays], core_ids=[0])
    return np.ascontiguousarray(r.results[0]["out_t"].reshape(D, SEQ).T).reshape(1, SEQ, D)
```

```python
from contextlib import ExitStack

import concourse.bass as bass
from concourse import mybir

F32 = mybir.dt.float32
F32R = mybir.dt.float32r
ALU = mybir.AluOpType
ACT = mybir.ActivationFunctionType
AX = mybir.AxisListType

P = 128
DEPTH = 2
SEQ = 512
D = 1024
KC = D // P
CHUNK = 64
NCH = SEQ // CHUNK
HD = 64
HQ = 8
NTOK = SEQ // P
GROUPS = 8
FF = 4 * D
QUARTERS = FF // D
EPS = 1e-6
GELU_C = 0.7978845608028654
GELU_A = 0.044715
LOWEST = -3.4028234663852886e38

GV_POS, K_POS, Q_POS, V_POS, U_POS, WO_POS, MLP_POS = 0, 4, 5, 9, 10, 14, 22
PER_QUARTER = 2 * KC
PER_LAYER = MLP_POS + QUARTERS * PER_QUARTER
SLOTS = 4
BANKS = 4
CREDIT = 4
OUT_BY_POOL = 3
POOL_STORES = [(0, 2), (2, 3)]
DVE_STORES = [(3, 4), (4, 6), (6, 7), (7, 8)]
FIRST_STORES = [(3, 4), (4, 6), (0, 2), (6, 7), (7, 8), (2, 3)]
HALF = SEQ // 2
WARM = 3
BY_POOL = 3


def slot_of(pos):
    return (pos - MLP_POS) % SLOTS


SLOT_USES = [sum(slot_of(i) == s for i in range(PER_LAYER)) for s in range(SLOTS)]


def landed_value(layer, pos):
    s = slot_of(pos)
    before = sum(slot_of(i) == s for i in range(pos))
    return (layer * SLOT_USES[s] + before + 1) * 16


def mlp_landed_value(quad, s):
    before = sum(slot_of(i) == s for i in range(MLP_POS))
    return (before + quad + 1) * 16


def before_in_slot(pos):
    s = slot_of(pos)
    back = [i for i in range(pos) if slot_of(i) == s]
    return back[-1] if back else max(i for i in range(PER_LAYER) if slot_of(i) == s) - PER_LAYER


FM_PER_LAYER = PER_LAYER - K_POS


def fm_of(pos):
    return pos - K_POS


def bank_of(fm):
    return (fm + 2) % BANKS


def before_in_bank(fm):
    if fm >= BANKS:
        return fm - BANKS
    return max(j for j in range(FM_PER_LAYER) if bank_of(j) == bank_of(fm)) - FM_PER_LAYER


C_ORDER = (0, 2, 1, 3)


def build(nc, x, gains, weights, sinks, ws, bs, alibi, ident_in, out):
    with ExitStack() as ctx:
        def sb(name, shape, dt=F32):
            return ctx.enter_context(nc.sbuf_tensor(name, shape, dt))

        def sem(name):
            return ctx.enter_context(nc.semaphore(name))

        raw = sb("raw", [P, SLOTS, D])
        whi = sb("whi", [P, SLOTS, D], F32R)
        wlo = sb("wlo", [P, SLOTS, D], F32R)
        xt = sb("xt", [P, KC, SEQ])
        xhi = sb("xhi", [P, KC, SEQ], F32R)
        xlo = sb("xlo", [P, KC, SEQ], F32R)
        ahi = sb("ahi", [P, KC, SEQ], F32R)
        alo = sb("alo", [P, KC, SEQ], F32R)
        sumsq = sb("sumsq", [P, SEQ])
        sq = sb("sq", [P, 2, SEQ])
        rbc = sb("rbc", [P, SEQ])
        diag = sb("diag", [P, NTOK, P])
        rcol = sb("rcol", [P, NTOK])
        kt = sb("kt", [P, CHUNK + SEQ])
        vt = sb("vt", [P, CHUNK + SEQ])
        qt = sb("qt", [P, NCH, 4, CHUNK])
        vband = sb("vband", [P, NCH, P])
        band = sb("band", [P, 4, NCH, P])
        negmax = sb("negmax", [P, 4, NCH])
        rowmax = sb("rowmax", [P, 4, NCH])
        sinkarg = sb("sinkarg", [P, 4, NCH])
        sinkexp = sb("sinkexp", [P, 4, NCH])
        den = sb("den", [P, 4, NCH])
        dsum = sb("dsum", [P, 4, NCH])
        rden = sb("rden", [P, 4, NCH])
        ut = sb("ut", [P, 4, SEQ])
        gv = sb("gv", [P, NTOK, SEQ])
        z = sb("z", [P, 2, SEQ])
        pp = sb("pp", [P, 2, SEQ])
        gsum = sb("gsum", [P, NTOK, GROUPS])
        gvar = sb("gvar", [P, NTOK, GROUPS])
        grstd = sb("grstd", [P, NTOK, GROUPS])
        wst = sb("wst", [P, GROUPS, P])
        bsb = sb("bsb", [P, 4, P])
        gain = sb("gain", [P, (2 * DEPTH + 1) * KC])
        sink = sb("sink", [P, DEPTH * 4])
        sink_now = sb("sink_now", [P, 4])
        bias = sb("bias", [P, 4, 2, P])
        ident = sb("ident", [P, P])
        ones = sb("ones", [P, P])
        eps = sb("eps", [P, 2])
        root = sb("root", [P, 1])
        zero = sb("zero", [P, 1])

        bank = [ctx.enter_context(nc.psum_tensor(f"bank{i}", [P, 512], F32)) for i in range(8)]

        raw_landed = [sem(f"raw_landed{s}") for s in range(SLOTS)]
        x_landed = [sem(f"x_landed{i}") for i in range(KC // 2 + 1)]
        gain_landed = sem("gain_landed")
        const_landed = sem("const_landed")
        gate_landed = sem("gate_landed")
        ones_set = sem("ones_set")
        zeros_set = sem("zeros_set")
        zero_set = sem("zero_set")
        whi_ready = sem("whi_ready")
        first_landed = sem("first_landed")
        first_ready = sem("first_ready")
        half_done = sem("half_done")
        half_taken = sem("half_taken")
        half_squared = sem("half_squared")
        half_summed = sem("half_summed")
        half_high = sem("half_high")
        diag_zeroed = sem("diag_zeroed")
        diag_ready = sem("diag_ready")
        r_filled = sem("r_filled")
        rbc_ready = sem("rbc_ready")
        rbc_inverted = sem("rbc_inverted")
        whi_by_pool = sem("whi_by_pool")
        wlo_ready = sem("wlo_ready")
        group_done = sem("group_done")
        evicted = sem("evicted")
        xhi_ready = sem("xhi_ready")
        xlo_ready = sem("xlo_ready")
        sq_ready = sem("sq_ready")
        sumsq_steps = sem("sumsq_steps")
        stat_filled = sem("stat_filled")
        std_ready = sem("std_ready")
        rcol_ready = sem("rcol_ready")
        scores_filled = sem("scores_filled")
        scores_taken = sem("scores_taken")
        sink_taken = sem("sink_taken")
        rowmax_ready = sem("rowmax_ready")
        negmax_ready = sem("negmax_ready")
        sinkarg_ready = sem("sinkarg_ready")
        exps_done = sem("exps_done")
        dsum_ready = sem("dsum_ready")
        rden_ready = sem("rden_ready")
        probs_ready = sem("probs_ready")
        vband_filled = sem("vband_filled")
        vband_taken = sem("vband_taken")
        pt_filled = sem("pt_filled")
        pt_taken = sem("pt_taken")
        pv_filled = sem("pv_filled")
        att_hi = sem("att_hi")
        att_lo = sem("att_lo")
        gv_done = sem("gv_done")
        square_ready = sem("square_ready")
        poly_ready = sem("poly_ready")
        tanh_ready = sem("tanh_ready")
        gelu_ready = sem("gelu_ready")
        gsum_ready = sem("gsum_ready")
        centred = sem("centred")
        csq_ready = sem("csq_ready")
        gvar_ready = sem("gvar_ready")
        gstd_ready = sem("gstd_ready")
        grstd_ready = sem("grstd_ready")
        vn_ready = sem("vn_ready")
        sgu_filled = sem("sgu_filled")
        sgu_taken = sem("sgu_taken")
        sgu_ready = sem("sgu_ready")
        sgu_hi = sem("sgu_hi")
        sgu_lo = sem("sgu_lo")
        hid_ready = sem("hid_ready")
        hid_hi = sem("hid_hi")
        hid_lo = sem("hid_lo")
        out_ready = sem("out_ready")
        out_by_pool = sem("out_by_pool")
        scaled_ready = sem("scaled_ready")
        out_stored = sem("out_stored")

        def sgu_bank(pr):
            return 4 + (pr + 2) % 4

        def mixbuf(pr):
            return (vt if pr % 2 else kt)[:, CHUNK:]

        def group_value(layer, pos):
            return layer * PER_LAYER + (pos + 1 + CREDIT)

        def evicted_value(layer, fm):
            return layer * FM_PER_LAYER + (fm + 1 + CREDIT)

        def final(m):
            return band[:, m // 2, (m % 2) * 4:(m % 2) * 4 + 4, :].rearrange("p n k -> p (n k)")

        def store(engine, a, b, h):
            tokens = slice(h * HALF, (h + 1) * HALF)
            src = band[:, :, :, :].rearrange("p c n k -> p (c n k)").rearrange("p (m t) -> p m t", t=SEQ)
            engine.dma_start(out[a:b, :, tokens].rearrange("m p t -> p m t"), src[:, a:b, tokens]) \
                .then_inc(out_stored, 16)

        block = ctx.enter_context(nc.Block())

        @block.sync
        def _(sp):
            def load(layer, pos, group):
                sp.wait_ge(wlo_ready, group_value(layer, before_in_slot(pos)))
                src = weights[bass.ds(group, 1)].rearrange("a p f -> (a p) f")
                first = 0
                if pos == 0:
                    first = D // 2
                    sp.dma_start(raw[:, slot_of(pos), 0:first], src[:, 0:first]).then_inc(first_landed, 16)
                sp.dma_start(raw[:, slot_of(pos), first:], src[:, first:]).then_inc(raw_landed[slot_of(pos)], 16)

            with sp.Fori(0, DEPTH) as l:
                for pos in range(MLP_POS):
                    load(l, pos, l * PER_LAYER + pos)
                    if pos == 3:
                        lo, hi = slice(0, CHUNK), slice(CHUNK, P)
                        wl = ws[bass.ds(l, 1)].rearrange("a j g i -> (a j) g i")
                        sp.dma_start(wst[lo, :, :], wl[lo, :, :]).then_inc(gate_landed, 16)
                        sp.dma_start(wst[hi, :, CHUNK:P], wl[hi, :, CHUNK:P]).then_inc(gate_landed, 16)
                        for r in range(2):
                            src = bs[bass.ds(l, 1), r].rearrange("a c i -> a (c i)").broadcast_to([HD, 4 * P])
                            sp.dma_start(bsb[r * HD:(r + 1) * HD, :, :].rearrange("p c i -> p (c i)"), src) \
                                .then_inc(gate_landed, 16)
                with sp.Fori(0, QUARTERS * PER_QUARTER // SLOTS) as quad:
                    for s in range(SLOTS):
                        sp.wait_ge(wlo_ready, l * PER_LAYER + quad * SLOTS + (MLP_POS + s - SLOTS + 1 + CREDIT))
                        group = l * PER_LAYER + quad * SLOTS + (MLP_POS + s)
                        sp.dma_start(raw[:, s, :], weights[bass.ds(group, 1)].rearrange("a p f -> (a p) f")) \
                            .then_inc(raw_landed[s], 16)
            for a, b in FIRST_STORES:
                if b <= OUT_BY_POOL:
                    sp.wait_ge(out_by_pool, b)
                else:
                    sp.wait_ge(out_ready, b - OUT_BY_POOL)
                store(sp, a, b, 0)
            for a, b in DVE_STORES:
                sp.wait_ge(out_ready, KC - OUT_BY_POOL + b - OUT_BY_POOL)
                store(sp, a, b, 1)
            sp.wait_ge(out_stored, 16 * 2 * len(POOL_STORES + DVE_STORES))

        @block.gpsimd
        def _(pool):
            pool.memset(zero[:, :], 0.0).then_inc(zero_set, 1)
            pool.memset(eps[:, 0:1], EPS)
            pool.memset(eps[:, 1:2], 4 * EPS).then_inc(wlo_ready, CREDIT)
            pool.wait_ge(zero_set, 1)

            def low(slot, cols, ready):
                pool.tensor_tensor(wlo[:, slot, cols], raw[:, slot, cols], whi[:, slot, cols], ALU.subtract) \
                    .then_inc(ready, 1)

            with pool.Fori(0, DEPTH) as l:
                for pos in range(MLP_POS):
                    s = slot_of(pos)
                    if pos < BY_POOL:
                        for h in range(2):
                            if pos == 0 and h == 0:
                                pool.wait_ge(first_landed, l * 16 + 16)
                            else:
                                pool.wait_ge(raw_landed[s], landed_value(l, pos))
                            if h == 0:
                                pool.wait_ge(group_done, group_value(l, before_in_slot(pos)))
                            cols = slice(h * (D // 2), (h + 1) * (D // 2))
                            pool.tensor_tensor(whi[:, s, cols], raw[:, s, cols],
                                               zero[:, :].broadcast_to([P, D // 2]), ALU.add) \
                                .then_inc(whi_by_pool, 1)
                            pool.wait_ge(whi_by_pool, l * (2 * BY_POOL) + (2 * pos + h + 1))
                            low(s, cols, wlo_ready if h else first_ready)
                    else:
                        pool.wait_ge(whi_ready, l * (PER_LAYER - BY_POOL) + (pos - BY_POOL + 1))
                        low(s, slice(0, D), wlo_ready)
                with pool.Fori(0, QUARTERS * PER_QUARTER // SLOTS) as quad:
                    for s in range(SLOTS):
                        pool.wait_ge(whi_ready, l * (PER_LAYER - BY_POOL) + quad * SLOTS + (MLP_POS + s - BY_POOL + 1))
                        low(s, slice(0, D), wlo_ready)
            for m in range(OUT_BY_POOL):
                g = gain[:, 2 * DEPTH * KC + m:2 * DEPTH * KC + m + 1]
                pool.wait_ge(evicted, evicted_value(DEPTH - 1, fm_of(PER_LAYER - KC + m)))
                pool.tensor_tensor(gv[:, m, :], xt[:, m, :], g.broadcast_to([P, SEQ]), ALU.mult).then_inc(scaled_ready, 1)
            for h in range(2):
                tokens = slice(h * HALF, (h + 1) * HALF)
                pool.wait_ge(rbc_ready, DEPTH + (h + 1))
                for m in range(OUT_BY_POOL):
                    pool.wait_ge(scaled_ready, m + 1)
                    pool.tensor_tensor(final(m)[:, tokens], gv[:, m, tokens], rbc[:, tokens], ALU.mult) \
                        .then_inc(out_by_pool, 1)

        @block.tensor
        def _(pe):
            def products(pos, lay, q, hi, lo, before_chunk=None, order=range(KC), tokens=slice(0, SEQ),
                         to=None, done=group_done):
                s = slot_of(pos)
                o = (bank[bank_of(fm_of(pos))] if to is None else to)[:, tokens]
                pe.wait_ge(wlo_ready, lay * PER_LAYER + q * PER_QUARTER + (pos + 1 + CREDIT))
                for kc in order:
                    if before_chunk:
                        before_chunk(kc)
                    wc = slice(kc * P, (kc + 1) * P)
                    pe.matmul(o, wlo[:, s, wc], hi[:, kc, tokens], start=(kc == order[0]), stop=False)
                    pe.matmul(o, whi[:, s, wc], hi[:, kc, tokens], start=False, stop=False)
                    mm = pe.matmul(o, whi[:, s, wc], lo[:, kc, tokens], start=False, stop=(kc == order[-1]))
                mm.then_inc(done, 1)

            def statistics(columns, tiles=range(NTOK)):
                for t in tiles:
                    mm = pe.matmul(columns[:, t:t + 1], sumsq[:, t * P:(t + 1) * P], ones[:, 0:1],
                                   start=True, stop=True)
                mm.then_inc(stat_filled, 1)

            def spread(count, row, tiles=range(NTOK)):
                for t in tiles:
                    pe.wait_ge(diag_ready, count * NTOK + (t + 1))
                    mm = pe.matmul(row[:, t * P:(t + 1) * P], ones[:, :], diag[:, t, :], start=True, stop=True)
                mm.then_inc(r_filled, 1)

            def bank_free(lay, fm):
                pe.wait_ge(evicted, evicted_value(lay, before_in_bank(fm)))

            pe.wait_ge(ones_set, 2)
            pe.wait_ge(diag_zeroed, 1)
            for i in range(WARM):
                pe.matmul(bank[7][:, :], ones[:, :], diag[:, :, :].rearrange("p t k -> p (t k)"),
                          start=True, stop=True)

            def keep_warm(count):
                for i in range(count):
                    pe.matmul(bank[4][:, 0:P], ones[:, :], ident[:, :], start=True, stop=True)

            with pe.Fori(0, DEPTH) as l:
                for s4 in range(4):
                    pos = GV_POS + s4
                    s = slot_of(pos)
                    steps = [(t, b) for b in range(2) for t in range(NTOK)]
                    if s4 == 3:
                        steps.sort()
                    for t, b in steps:
                        tok = slice(t * P, (t + 1) * P)
                        kc, wc = 2 * s4 + b, slice(b * 512, (b + 1) * 512)
                        if pos < BY_POOL and b == 0 and t == 0:
                            pe.wait_ge(first_ready, l * BY_POOL + (pos + 1))
                        elif t == 0:
                            pe.wait_ge(wlo_ready, group_value(l, pos))
                        if t == 0:
                            pe.wait_ge(xlo_ready, l * (2 * KC) + (kc + 1))
                            if kc == 0:
                                pe.wait_ge(half_taken, l + 1)
                        o = bank[4 + t][:, :]
                        pe.matmul(o, xhi[:, kc, tok], wlo[:, s, wc], start=(kc == 0), stop=False)
                        pe.matmul(o, xhi[:, kc, tok], whi[:, s, wc], start=False, stop=False)
                        mm = pe.matmul(o, xlo[:, kc, tok], whi[:, s, wc], start=False, stop=(kc == KC - 1))
                        if s4 == 3 and b == 1 and t < NTOK - 1:
                            mm.then_inc(gv_done, 1)
                    mm.then_inc(group_done, 1)

                bank_free(l, 3)
                pe.wait_ge(sumsq_steps, 2 * l * (KC - 1) + (KC - 1))
                statistics(bank[1])

                def project(pos, before_chunk=None):
                    fm = fm_of(pos)
                    if fm in (2, 3):
                        pe.wait_ge(rbc_ready, l + 1)
                    else:
                        bank_free(l, fm)
                    products(pos, l, 0, xhi, xlo, before_chunk)

                def scores(tp):
                    pe.wait_ge(evicted, evicted_value(l, fm_of(Q_POS) + 2 * tp + 1))
                    for nh in range(2):
                        f = 4 * tp + 2 + nh
                        if f < 4:
                            pe.wait_ge(square_ready, l * 8 + (f + 1))
                        else:
                            pe.wait_ge(scores_taken, l * 8 + (f - 4 + 1))
                        for n in range(4 * nh, 4 * nh + 4):
                            for half in range(2):
                                part = slice(half * HD, (half + 1) * HD)
                                mm = pe.matmul(bank[4 + 2 * half + nh][:, (n % 4) * P:(n % 4 + 1) * P],
                                               qt[part, n, 2 * tp:2 * tp + 2, :].rearrange("p t q -> p (t q)"),
                                               kt[part, n * CHUNK:n * CHUNK + P], start=True, stop=True)
                        mm.then_inc(scores_filled, 1)

                def turn_probs(ci):
                    c = C_ORDER[ci]
                    pe.wait_ge(probs_ready, l * 4 + (ci + 1))
                    for nh in range(2):
                        f = 2 * ci + nh
                        if ci == 0:
                            pe.wait_ge(scores_taken, l * 8 + (6 + nh + 1))
                        elif ci == 1:
                            pe.wait_ge(vband_taken, l * 2 + (nh + 1))
                        else:
                            pe.wait_ge(sgu_taken, l * 4 + (f - 4 + 1))
                        for n in range(4 * nh, 4 * nh + 4):
                            mm = pe.transpose(bank[4 + (f + 2) % 4][:, (n % 4) * P:(n % 4 + 1) * P],
                                              band[:, c, n, :], ident[:, :])
                        mm.then_inc(pt_filled, 1)

                project(K_POS)
                spread(l, bank[0])
                project(Q_POS)
                project(Q_POS + 1)
                project(Q_POS + 2)
                scores(0)
                project(Q_POS + 3)
                project(V_POS)
                scores(1)
                project(U_POS)
                pe.wait_ge(const_landed, 16 * 4)
                pe.wait_ge(evicted, evicted_value(l, fm_of(V_POS)))
                for nh in range(2):
                    pe.wait_ge(scores_taken, l * 8 + (4 + nh + 1))
                    for n in range(4 * nh, 4 * nh + 4):
                        mm = pe.transpose(bank[4 + nh][:, (n % 4) * P:(n % 4 + 1) * P],
                                          vt[:, n * CHUNK:n * CHUNK + P], ident[:, :])
                    mm.then_inc(vband_filled, 1)
                project(U_POS + 1)
                turn_probs(0)
                turn_probs(1)
                project(U_POS + 2)

                def mix_positions(pr):
                    pe.wait_ge(pt_taken, l * 8 + (pr + 1))
                    for t in range(NTOK):
                        for r in range(2):
                            g = 2 * pr + r
                            mm = pe.matmul(bank[sgu_bank(pr)][r * HD:(r + 1) * HD, t * P:(t + 1) * P],
                                           gv[:, t, g * HD:(g + 1) * HD], wst[:, g, :], start=True, stop=True)
                    mm.then_inc(sgu_filled, 1)

                pe.wait_ge(gate_landed, l * 64 + 64)
                pe.wait_ge(zeros_set, 1)
                pe.wait_ge(vn_ready, l * 4 + 4)
                for pr in range(4):
                    mix_positions(pr)

                def turn_others(kc):
                    if kc == 2:
                        turn_probs(2)
                    if kc == 5:
                        turn_probs(3)

                project(U_POS + 3, turn_others)

                pe.wait_ge(pt_taken, l * 8 + 8)
                for b in range(4):
                    for n in range(2 * b, 2 * b + 2):
                        for half in range(2):
                            part = slice(half * HD, (half + 1) * HD)
                            mm = pe.matmul(bank[4 + b][part, (n % 2) * 256:(n % 2 + 1) * 256],
                                           vband[:, n, part], band[:, 2 * half:2 * half + 2, n, :],
                                           start=True, stop=True)
                    mm.then_inc(pv_filled, 1)

                def mixed(kc):
                    if kc == 0:
                        pe.wait_ge(att_lo, l * 4 + 4)
                    if kc >= 4:
                        pe.wait_ge(sgu_lo, l * 4 + (kc - 4 + 1))

                for m in range(KC):
                    pos = WO_POS + m
                    bank_free(l, fm_of(pos))
                    products(pos, l, 0, ahi, alo, mixed if m == 0 else None, order=(4, 5, 6, 0, 1, 2, 3, 7))

                def mlp_group(q, pos, hi, lo, before_chunk=None, tokens=slice(0, SEQ)):
                    pe.wait_ge(evicted, l * FM_PER_LAYER + q * PER_QUARTER + (fm_of(pos) - BANKS + 1 + CREDIT))
                    products(pos, l, q, hi, lo, before_chunk, tokens=tokens)

                def rest_of_quarter(q, last):
                    for m in range(1, KC):
                        mlp_group(q, MLP_POS + m, xhi, xlo)
                    for m in range(KC - 1 if last else KC):
                        mlp_group(q, MLP_POS + KC + m, ahi, alo,
                                  (lambda kc: pe.wait_ge(hid_lo, l * (QUARTERS * KC) + q * KC + (kc + 1)))
                                  if m == 0 else None)
                    if last:
                        pos = MLP_POS + PER_QUARTER - 1
                        products(pos, l, q, ahi, alo, tokens=slice(0, HALF), to=bank[4], done=half_done)
                        mlp_group(q, pos, ahi, alo, tokens=slice(HALF, SEQ))

                def first_up(kc):
                    pe.wait_ge(xlo_ready, l * (2 * KC) + (KC + kc + 1))

                mlp_group(0, MLP_POS, xhi, xlo, first_up)
                pe.wait_ge(sumsq_steps, (2 * l + 1) * (KC - 1) + (KC - 1))
                pe.matmul(bank[4][:, :], ones[:, :], sumsq[:, :], start=True, stop=True).then_inc(stat_filled, 1)
                with pe.Fori(0, QUARTERS - 1) as q:
                    rest_of_quarter(q, False)
                    mlp_group(q, MLP_POS + PER_QUARTER, xhi, xlo)
                rest_of_quarter(QUARTERS - 1, True)

            first, second = (0, 1), (2, 3)
            pe.wait_ge(half_summed, DEPTH)
            statistics(bank[5], first)
            keep_warm(5)
            pe.wait_ge(sumsq_steps, (2 * DEPTH + 1) * (KC - 1))
            statistics(bank[7], second)
            spread(DEPTH, bank[6], first)
            keep_warm(1)
            spread(DEPTH, bank[5], second)

        @block.scalar
        def _(act):
            def high(l, pos, q=0):
                s = slot_of(pos)
                if pos < MLP_POS:
                    act.wait_ge(raw_landed[s], landed_value(l, pos))
                    act.wait_ge(group_done, group_value(l, before_in_slot(pos)))
                else:
                    k = pos - MLP_POS
                    act.wait_ge(raw_landed[s], l * (16 * SLOT_USES[s]) + q * (16 * PER_QUARTER // SLOTS)
                                + mlp_landed_value(k // SLOTS, s))
                    act.wait_ge(group_done, l * PER_LAYER + q * PER_QUARTER
                                + (pos - SLOTS + 1 + CREDIT))
                act.activation(whi[:, s, :], raw[:, s, :], ACT.Copy).then_inc(whi_ready, 1)

            def norm_chunk(norm, m, gain_col):
                act.mul(xhi[:, m, :], xt[:, m, :], gain_col).then_inc(xhi_ready, 1)
                dst = sumsq[:, :] if m == 0 else sq[:, m % 2, :]
                if m >= 3:
                    act.wait_ge(sumsq_steps, norm * (KC - 1) + (m - 2))
                act.activation(dst, xt[:, m, :], ACT.Square).then_inc(sq_ready, 1)

            def last_chunk_high(tokens, gain_col, ready):
                act.mul(xhi[:, KC - 1, tokens], xt[:, KC - 1, tokens], gain_col).then_inc(ready, 1)

            def std(norm, columns):
                act.activation(root[:, :], eps[:, 0:1], ACT.Sqrt)
                act.wait_ge(stat_filled, norm + 1)
                act.activation(rcol[:, :], columns[:, 0:NTOK], ACT.Sqrt, scale=1.0 / D, bias=eps[:, 0:1]) \
                    .then_inc(std_ready, 1)

            def take_spread(count, row):
                act.wait_ge(r_filled, count + 1)
                act.copy(rbc[:, :], row[:, :]).then_inc(rbc_ready, 1)

            act.dma_start(xt[:, 0, :], x[0]).then_inc(x_landed[0], 16)
            act.dma_start(gain[:, :], gains).then_inc(gain_landed, 16)
            act.dma_start(xt[:, 1, :], x[1]).then_inc(x_landed[1], 16)
            act.wait_ge(wlo_ready, CREDIT)
            act.activation(root[:, :], eps[:, 0:1], ACT.Square)
            for m in range(2, KC, 2):
                act.dma_start(xt[:, m:m + 2, :], x[m:m + 2].rearrange("m p t -> p m t")).then_inc(x_landed[m // 2 + 1], 16)
            act.wait_ge(gain_landed, 16)
            for m in range(KC):
                act.wait_ge(x_landed[m // 2 + 1 if m else 0], 16)
                if m < KC - 1:
                    norm_chunk(0, m, gain[:, m:m + 1])
            last_chunk_high(slice(0, HALF), gain[:, KC - 1:KC], half_high)
            act.wait_ge(sumsq_steps, KC - 3)
            act.activation(sq[:, (KC - 1) % 2, :], xt[:, KC - 1, :], ACT.Square).then_inc(sq_ready, 1)
            act.dma_start(ident[:, :], ident_in).then_inc(const_landed, 16)
            act.dma_start(bias[:, :, :, :].rearrange("p c a k -> p (c a k)"), alibi).then_inc(const_landed, 16)
            for r in range(2):
                src = sinks[:, r].rearrange("(a l) c -> a (l c)", a=1).broadcast_to([HD, DEPTH * 4])
                act.dma_start(sink[r * HD:(r + 1) * HD, :], src).then_inc(const_landed, 16)

            with act.Fori(0, DEPTH) as l:
                def softmax(ci):
                    c = C_ORDER[ci]
                    act.wait_ge(negmax_ready, l * 4 + (ci + 1))
                    for n in range(NCH):
                        act.activation(band[:, c, n, :], band[:, c, n, :], ACT.Exp, bias=negmax[:, c, n:n + 1],
                                       accum_out=den[:, c, n:n + 1])
                    act.wait_ge(sinkarg_ready, l * 4 + (ci + 1))
                    act.activation(sinkexp[:, c, :], sinkarg[:, c, :], ACT.Exp).then_inc(exps_done, 1)

                def square_gate(t):
                    if t < NTOK - 1:
                        act.wait_ge(gv_done, l * 3 + (t + 1))
                    else:
                        act.wait_ge(group_done, group_value(l, GV_POS + 3))
                    if t >= 2:
                        act.wait_ge(gelu_ready, l * 8 + (t - 1))
                    act.mul(z[:, t % 2, :], bank[4 + t][:, :], rcol[:, t:t + 1])
                    act.activation(pp[:, t % 2, :], bank[4 + t][:, :], ACT.Square, scale=rcol[:, t:t + 1]) \
                        .then_inc(square_ready, 1)

                def tanh(k):
                    act.wait_ge(poly_ready, l * 8 + (k + 1))
                    act.activation(pp[:, k % 2, :], pp[:, k % 2, :], ACT.Tanh, scale=GELU_C * GELU_A) \
                        .then_inc(tanh_ready, 1)

                def centred_square(t):
                    act.wait_ge(centred, l * 4 + (t + 1))
                    if t >= 2:
                        act.wait_ge(gvar_ready, l * 4 + (t - 1))
                    act.activation(sq[:, t % 2, :], gv[:, t, :], ACT.Square).then_inc(csq_ready, 1)

                def take_turned(ci):
                    c = C_ORDER[ci]
                    for f in range(2 * ci, 2 * ci + 2):
                        act.wait_ge(pt_filled, l * 8 + (f + 1))
                        act.copy(band[:, c, 4 * (f % 2):4 * (f % 2) + 4, :],
                                 bank[4 + (f + 2) % 4][:, :].rearrange("p (n k) -> p n k", n=4)).then_inc(pt_taken, 1)

                def product_high(pr):
                    act.wait_ge(sgu_ready, l * 4 + (pr + 1))
                    act.copy(ahi[:, 4 + pr, :], sq[:, pr % 2, :]).then_inc(sgu_hi, 1)

                def gelu_square(c):
                    act.wait_ge(evicted, evicted_value(l, fm_of(U_POS) + c))
                    act.wait_ge(gelu_ready, l * 8 + (c + 3))
                    act.activation(pp[:, c % 2, :], z[:, c % 2, :], ACT.Square).then_inc(square_ready, 1)

                def gelu_u(c):
                    gelu_square(c)
                    tanh(4 + c)

                last_chunk_high(slice(HALF, SEQ), gain[:, bass.ds(l * (2 * KC) + (KC - 1), 1)], xhi_ready)
                for pos in range(3, 7):
                    high(l, pos)
                std(2 * l, bank[1])
                high(l, 7)
                act.wait_ge(rcol_ready, l + 1)
                square_gate(0)
                square_gate(1)
                tanh(0)
                take_spread(l, bank[0])
                high(l, 8)
                square_gate(2)
                tanh(1)
                centred_square(0)
                high(l, 9)
                square_gate(3)
                tanh(2)
                centred_square(1)
                tanh(3)
                centred_square(2)
                high(l, 10)
                centred_square(3)
                act.wait_ge(gvar_ready, l * 4 + 4)
                act.activation(grstd[:, :, :], gvar[:, :, :], ACT.Sqrt, scale=1.0 / HD, bias=eps[:, 1:2]) \
                    .then_inc(gstd_ready, 1)
                high(l, 11)
                softmax(0)
                high(l, 12)
                softmax(1)
                high(l, 13)
                softmax(2)
                high(l, 14)
                for nh in range(2):
                    act.wait_ge(vband_filled, l * 2 + (nh + 1))
                    act.copy(vband[:, 4 * nh:4 * nh + 4, :],
                             bank[4 + nh][:, :].rearrange("p (n k) -> p n k", n=4)).then_inc(vband_taken, 1)
                gelu_u(0)
                softmax(3)
                high(l, 15)
                gelu_u(1)
                take_turned(0)
                take_turned(1)
                high(l, 16)
                gelu_u(2)
                product_high(0)
                product_high(1)
                take_turned(2)
                take_turned(3)
                product_high(2)

                def attended_high(b):
                    act.wait_ge(pv_filled, l * 4 + (b + 1))
                    act.copy(ahi[:, 0:4, b * P:(b + 1) * P].rearrange("p t (n q) -> p t n q", n=2),
                             bank[4 + b][:, :].rearrange("p (n t q) -> p t n q", n=2, t=4)).then_inc(att_hi, 1)

                gelu_square(3)
                attended_high(0)
                tanh(7)
                attended_high(1)
                attended_high(2)
                attended_high(3)
                product_high(3)
                high(l, 17)

                for m in range(KC):
                    act.wait_ge(evicted, evicted_value(l, fm_of(WO_POS + m)))
                    norm_chunk(2 * l + 1, m, gain[:, bass.ds(l * (2 * KC) + (KC + m), 1)])
                    high(l, WO_POS + m + 4)

                def hidden_high(q, m):
                    act.wait_ge(hid_ready, l * (QUARTERS * KC) + q * KC + (m + 1))
                    act.copy(ahi[:, m % KC, :], pp[:, m % 2, :]).then_inc(hid_hi, 1)
                    high(l, MLP_POS + m + 4, q)

                def last_chunk_square(tokens, squared):
                    act.wait_ge(sumsq_steps, (2 * l + 2) * (KC - 1) + (KC - 3))
                    act.activation(sq[:, (KC - 1) % 2, tokens], xt[:, KC - 1, tokens], ACT.Square).then_inc(squared, 1)

                def rest_of_quarter(q, last):
                    for m in range(1, KC):
                        hidden_high(q, m)
                    for m in range(KC):
                        if last:
                            if m == KC - 1:
                                act.wait_ge(half_taken, l + 2)
                                last_chunk_square(slice(0, HALF), half_squared)
                                last_chunk_high(slice(0, HALF), gain[:, bass.ds(l * (2 * KC) + (2 * KC + m), 1)], half_high)
                                act.wait_ge(evicted, evicted_value(l, FM_PER_LAYER - 1))
                                last_chunk_square(slice(HALF, SEQ), sq_ready)
                                continue
                            act.wait_ge(evicted, l * FM_PER_LAYER + q * PER_QUARTER
                                        + (fm_of(MLP_POS + KC + m) + 1 + CREDIT))
                            norm_chunk(2 * l + 2, m, gain[:, bass.ds(l * (2 * KC) + (2 * KC + m), 1)])
                        if not last or m < KC - 4:
                            high(l, MLP_POS + KC + m + 4, q)

                def next_first(q):
                    act.wait_ge(hid_ready, l * (QUARTERS * KC) + q * KC + (KC + 1))
                    act.copy(ahi[:, 0, :], pp[:, 0, :]).then_inc(hid_hi, 1)
                    high(l, MLP_POS + PER_QUARTER + 4, q)

                act.activation(root[:, :], eps[:, 0:1], ACT.Sqrt)
                act.wait_ge(stat_filled, 2 * l + 2)
                act.activation(rbc[:, :], bank[4][:, :], ACT.Sqrt, scale=1.0 / D, bias=eps[:, 0:1]) \
                    .then_inc(std_ready, 1)
                hidden_high(0, 0)
                with act.Fori(0, QUARTERS - 1) as q:
                    rest_of_quarter(q, False)
                    next_first(q)
                rest_of_quarter(QUARTERS - 1, True)
            for h in range(2):
                tiles = slice(h * NTOK // 2, (h + 1) * NTOK // 2)
                act.wait_ge(stat_filled, 2 * DEPTH + (h + 1))
                act.activation(rcol[:, tiles], bank[7 if h else 5][:, tiles], ACT.Sqrt, scale=1.0 / D, bias=eps[:, 0:1]) \
                    .then_inc(std_ready, 1)
            for h in range(2):
                tokens = slice(h * HALF, (h + 1) * HALF)
                act.wait_ge(r_filled, DEPTH + (h + 1))
                act.copy(rbc[:, tokens], bank[5 if h else 6][:, tokens]).then_inc(rbc_ready, 1)
            for a, b in POOL_STORES:
                act.wait_ge(out_by_pool, OUT_BY_POOL + b)
                store(act, a, b, 1)

        @block.vector
        def _(dve):
            def norm_low(norm, m, gain_col):
                dve.wait_ge(xhi_ready, norm * KC + (m + 1))
                dve.scalar_tensor_tensor(xlo[:, m, :], xt[:, m, :], gain_col, xhi[:, m, :],
                                         ALU.mult, ALU.subtract).then_inc(xlo_ready, 1)

            def last_chunk_low(tokens, gain_col):
                return dve.scalar_tensor_tensor(xlo[:, KC - 1, tokens], xt[:, KC - 1, tokens], gain_col,
                                                xhi[:, KC - 1, tokens], ALU.mult, ALU.subtract)

            def add_square(norm, m):
                if m >= 1:
                    dve.wait_ge(sq_ready, norm * KC + (m + 1))
                    if m >= 2:
                        dve.wait_ge(sumsq_steps, norm * (KC - 1) + (m - 1))
                    dve.tensor_tensor(sumsq[:, :], sumsq[:, :], sq[:, m % 2, :], ALU.add).then_inc(sumsq_steps, 1)

            def rms(count):
                dve.wait_ge(std_ready, 2 * count + 1)
                dve.reciprocal(rcol[:, :], rcol[:, :]).then_inc(rcol_ready, 1)
                dve.wait_ge(rcol_ready, count + 1)
                for t in range(NTOK):
                    dve.tensor_scalar(diag[:, t, :], ident[:, :], rcol[:, t:t + 1], None, ALU.mult) \
                        .then_inc(diag_ready, 1)

            dve.memset(wst[P // 2:P, :, 0:P // 2], 0.0).then_inc(zeros_set, 1)
            dve.memset(diag[:, :, :], 0.0).then_inc(diag_zeroed, 1)
            dve.memset(ones[:, :], 1.0).then_inc(ones_set, 1)
            dve.memset(negmax[:, :, :], 0.0).then_inc(half_taken, 1)
            dve.memset(kt[:, 0:CHUNK], 0.0).then_inc(ones_set, 1)
            dve.memset(vt[:, 0:CHUNK], 0.0).then_inc(group_done, CREDIT)
            dve.memset(sinkarg[:, :, :], 0.0).then_inc(evicted, CREDIT)
            dve.wait_ge(gain_landed, 16)
            for m in range(KC):
                dve.wait_ge(x_landed[m // 2 + 1 if m else 0], 16)
                if m < KC - 1:
                    norm_low(0, m, gain[:, m:m + 1])
                else:
                    dve.wait_ge(half_high, 1)
                    last_chunk_low(slice(0, HALF), gain[:, m:m + 1])
                add_square(0, m)
            dve.wait_ge(const_landed, 16 * 4)

            with dve.Fori(0, DEPTH) as l:
                def scaled(pos, dst):
                    by_chunk = lambda ap: ap.rearrange("p (n q) -> p n q", n=NCH)
                    dve.wait_ge(group_done, group_value(l, pos))
                    dve.tensor_tensor(dst, by_chunk(bank[bank_of(fm_of(pos))][:, :]), by_chunk(rbc[:, :]),
                                      ALU.mult).then_inc(evicted, 1)

                def scores(ci):
                    c = C_ORDER[ci]
                    for f in range(2 * ci, 2 * ci + 2):
                        dve.wait_ge(scores_filled, l * 4 + (2 * (f // 4) + f % 2 + 1))
                        src = bank[4 + f % 4]
                        first = 1 if f % 2 == 0 else 0
                        if first:
                            dve.scalar_tensor_tensor(band[:, c, 0, :], src[:, 0:P], HD ** -0.5, bias[:, c, 1, :],
                                                     ALU.mult, ALU.add)
                        n0 = 4 * (f % 2)
                        dve.scalar_tensor_tensor(
                            band[:, c, n0 + first:n0 + 4, :],
                            src[:, first * P:].rearrange("p (n k) -> p n k", k=P), HD ** -0.5,
                            bias[:, c, 0:1, :].broadcast_to([P, 4 - first, P]), ALU.mult, ALU.add) \
                            .then_inc(scores_taken, 1)
                    dve.wait_ge(scores_taken, l * 8 + (2 * ci + 2))
                    dve.tensor_reduce(rowmax[:, c, :], band[:, c, :, :], AX.X, ALU.max).then_inc(rowmax_ready, 1)
                    dve.wait_ge(rowmax_ready, l * 4 + (ci + 1))
                    s_col = sink_now[:, c:c + 1]
                    dve.tensor_scalar(negmax[:, c, :], rowmax[:, c, :], s_col, -1.0, ALU.max, ALU.mult) \
                        .then_inc(negmax_ready, 1)
                    dve.wait_ge(negmax_ready, l * 4 + (ci + 1))
                    dve.tensor_scalar(sinkarg[:, c, :], negmax[:, c, :], s_col, None, ALU.add).then_inc(sinkarg_ready, 1)

                def normalise(ci):
                    c = C_ORDER[ci]
                    dve.wait_ge(exps_done, l * 4 + (ci + 1))
                    dve.tensor_tensor(dsum[:, c, :], den[:, c, :], sinkexp[:, c, :], ALU.add).then_inc(dsum_ready, 1)
                    dve.wait_ge(dsum_ready, l * 4 + (ci + 1))
                    dve.reciprocal(rden[:, c, :], dsum[:, c, :]).then_inc(rden_ready, 1)
                    dve.wait_ge(rden_ready, l * 4 + (ci + 1))
                    dve.tensor_tensor(band[:, c, :, :], band[:, c, :, :],
                                      rden[:, c, :].rearrange("p (n a) -> p n a", a=1).broadcast_to([P, NCH, P]),
                                      ALU.mult).then_inc(probs_ready, 1)

                def poly(k):
                    dve.wait_ge(square_ready, l * 8 + (k + 1))
                    dve.scalar_tensor_tensor(pp[:, k % 2, :], pp[:, k % 2, :], 1.0 / GELU_A, z[:, k % 2, :],
                                             ALU.add, ALU.mult).then_inc(poly_ready, 1)

                def gate(k, dst):
                    dve.wait_ge(tanh_ready, l * 8 + (k + 1))
                    dve.scalar_tensor_tensor(dst, pp[:, k % 2, :], 1.0, z[:, k % 2, :],
                                             ALU.add, ALU.mult).then_inc(gelu_ready, 1)

                def by_group(ap):
                    return ap.rearrange("p (g c) -> p g c", g=GROUPS)

                def centre(t):
                    dve.wait_ge(gelu_ready, l * 8 + (t + 1))
                    dve.tensor_reduce(gsum[:, t, :], by_group(gv[:, t, :]), AX.X, ALU.add).then_inc(gsum_ready, 1)
                    dve.wait_ge(gsum_ready, l * 4 + (t + 1))
                    dve.scalar_tensor_tensor(
                        by_group(gv[:, t, :]), gsum[:, t, :].rearrange("p (g a) -> p g a", a=1).broadcast_to([P, GROUPS, HD]),
                        -1.0 / HD, by_group(gv[:, t, :]), ALU.mult, ALU.add).then_inc(centred, 1)

                def variance(t):
                    dve.wait_ge(csq_ready, l * 4 + (t + 1))
                    dve.tensor_reduce(gvar[:, t, :], by_group(sq[:, t % 2, :]), AX.X, ALU.add).then_inc(gvar_ready, 1)

                def normed_gates():
                    dve.wait_ge(gstd_ready, l + 1)
                    dve.reciprocal(grstd[:, :, :], grstd[:, :, :]).then_inc(grstd_ready, 1)
                    dve.wait_ge(grstd_ready, l + 1)
                    for t in range(NTOK):
                        dve.tensor_tensor(by_group(gv[:, t, :]), by_group(gv[:, t, :]),
                                          grstd[:, t, :].rearrange("p (g a) -> p g a", a=1).broadcast_to([P, GROUPS, HD]),
                                          ALU.mult).then_inc(vn_ready, 1)

                def take(ap):
                    return ap.rearrange("p (n q) -> p n q", n=NCH)

                dve.tensor_copy(sink_now[:, :], sink[:, bass.ds(l * 4, 4)]).then_inc(sink_taken, 1)
                dve.wait_ge(xhi_ready, l * (2 * KC) + KC)
                last_chunk_low(slice(HALF, SEQ), gain[:, bass.ds(l * (2 * KC) + (KC - 1), 1)]).then_inc(xlo_ready, 1)
                rms(l)
                dve.wait_ge(sink_taken, l + 1)
                poly(0)
                poly(1)
                gate(0, gv[:, 0, :])
                centre(0)
                dve.wait_ge(rbc_ready, l + 1)
                scaled(K_POS, take(kt[:, CHUNK:]))
                poly(2)
                gate(1, gv[:, 1, :])
                variance(0)
                centre(1)
                scaled(Q_POS, qt[:, :, 0, :])
                poly(3)
                gate(2, gv[:, 2, :])
                variance(1)
                centre(2)
                gate(3, gv[:, 3, :])
                variance(2)
                centre(3)
                scaled(Q_POS + 1, qt[:, :, 1, :])
                variance(3)
                scaled(Q_POS + 2, qt[:, :, 2, :])
                normed_gates()
                scores(0)
                scores(1)
                scaled(Q_POS + 3, qt[:, :, 3, :])
                normalise(0)
                scaled(V_POS, take(vt[:, CHUNK:]))
                normalise(1)
                scores(2)
                scores(3)
                normalise(2)
                scaled(U_POS, take(z[:, 0, :]))
                poly(4)
                gate(4, ut[:, 0, :])
                normalise(3)
                scaled(U_POS + 1, take(z[:, 1, :]))
                poly(5)
                gate(5, ut[:, 1, :])
                scaled(U_POS + 2, take(z[:, 0, :]))
                poly(6)
                gate(6, ut[:, 2, :])

                def sgu_low(pr):
                    dve.wait_ge(sgu_hi, l * 4 + (pr + 1))
                    dve.tensor_tensor(alo[:, 4 + pr, :], sq[:, pr % 2, :], ahi[:, 4 + pr, :], ALU.subtract) \
                        .then_inc(sgu_lo, 1)

                def mixed(pr):
                    dve.wait_ge(sgu_filled, l * 4 + (pr + 1))
                    if pr >= 2:
                        dve.wait_ge(sgu_ready, l * 4 + (pr - 1))
                    dve.tensor_tensor(mixbuf(pr).rearrange("p (t i) -> p t i", t=NTOK),
                                      bank[sgu_bank(pr)][:, :].rearrange("p (t i) -> p t i", t=NTOK),
                                      bsb[:, pr:pr + 1, :].broadcast_to([P, NTOK, P]), ALU.add).then_inc(sgu_taken, 1)

                def product(pr):
                    dve.wait_ge(gelu_ready, l * 8 + (4 + pr + 1))
                    dve.wait_ge(sgu_taken, l * 4 + (pr + 1))
                    if pr >= 2:
                        dve.wait_ge(sgu_lo, l * 4 + (pr - 1))
                    dve.scalar_tensor_tensor(sq[:, pr % 2, :], mixbuf(pr), 0.5, ut[:, pr, :],
                                             ALU.mult, ALU.mult).then_inc(sgu_ready, 1)

                def attended_low(b):
                    dve.wait_ge(att_hi, l * 4 + (b + 1))
                    a = slice(b * P, (b + 1) * P)
                    dve.tensor_tensor(alo[:, 0:4, a].rearrange("p t (n q) -> p t n q", n=2),
                                      bank[4 + b][:, :].rearrange("p (n t q) -> p t n q", n=2, t=4),
                                      ahi[:, 0:4, a].rearrange("p t (n q) -> p t n q", n=2),
                                      ALU.subtract).then_inc(att_lo, 1)

                mixed(0)
                mixed(1)
                product(0)
                product(1)
                mixed(2)
                mixed(3)
                sgu_low(0)
                sgu_low(1)
                product(2)
                scaled(U_POS + 3, take(z[:, 1, :]))
                sgu_low(2)
                poly(7)
                attended_low(0)
                gate(7, ut[:, 3, :])
                attended_low(1)
                attended_low(2)
                attended_low(3)
                product(3)
                sgu_low(3)

                def residual(q, pos, m):
                    dve.wait_ge(group_done, l * PER_LAYER + q * PER_QUARTER + (pos + 1 + CREDIT))
                    dve.tensor_tensor(xt[:, m, :], bank[bank_of(fm_of(pos))][:, :], xt[:, m, :], ALU.add) \
                        .then_inc(evicted, 1)

                def ffn_low(m):
                    norm_low(2 * l + 1, m, gain[:, bass.ds(l * (2 * KC) + (KC + m), 1)])

                def next_norm(m):
                    add_square(2 * l + 2, m)
                    norm_low(2 * l + 2, m, gain[:, bass.ds(l * (2 * KC) + (2 * KC + m), 1)])

                for m in range(KC):
                    residual(0, WO_POS + m, m)
                    ffn_low(m)
                    add_square(2 * l + 1, m)

                def hidden_low(q, m):
                    dve.wait_ge(hid_hi, l * (QUARTERS * KC) + q * KC + (m + 1))
                    dve.tensor_tensor(alo[:, m % KC, :], pp[:, m % 2, :], ahi[:, m % KC, :], ALU.subtract) \
                        .then_inc(hid_lo, 1)

                def hidden(q, m, low_before=None):
                    pos = MLP_POS + m if m < KC else MLP_POS + PER_QUARTER
                    dve.wait_ge(group_done, l * PER_LAYER + q * PER_QUARTER + (pos + 1 + CREDIT))
                    dve.tensor_tensor(z[:, m % 2, :], bank[bank_of(fm_of(pos))][:, :], rbc[:, :], ALU.mult) \
                        .then_inc(evicted, 1)
                    if low_before is not None:
                        hidden_low(q, low_before)
                    dve.wait_ge(evicted, l * FM_PER_LAYER + q * PER_QUARTER + (fm_of(pos) + 1 + CREDIT))
                    dve.scalar_tensor_tensor(pp[:, m % 2, :], z[:, m % 2, :], 0.0, z[:, m % 2, :],
                                             ALU.max, ALU.mult).then_inc(hid_ready, 1)

                def rest_of_quarter(q, last):
                    for m in range(1, KC):
                        hidden(q, m, m - 1)
                    hidden_low(q, KC - 1)
                    for m in range(KC - 1 if last else KC):
                        residual(q, MLP_POS + KC + m, m)
                        if last:
                            next_norm(m)
                    if last:
                        m, n = KC - 1, 2 * l + 2
                        g = gain[:, bass.ds(l * (2 * KC) + (2 * KC + m), 1)]
                        for h in range(2):
                            t = slice(h * HALF, (h + 1) * HALF)
                            if h == 0:
                                dve.wait_ge(half_done, l + 1)
                            else:
                                dve.wait_ge(group_done, group_value(l, PER_LAYER - 1))
                            dve.tensor_tensor(xt[:, m, t], (bank[bank_of(FM_PER_LAYER - 1)] if h else bank[4])[:, t],
                                              xt[:, m, t], ALU.add).then_inc(evicted if h else half_taken, 1)
                            if h == 0:
                                dve.wait_ge(half_squared, l + 1)
                            else:
                                dve.wait_ge(sq_ready, n * KC + (m + 1))
                            dve.wait_ge(sumsq_steps, n * (KC - 1) + (m - 1))
                            dve.tensor_tensor(sumsq[:, t], sumsq[:, t], sq[:, m % 2, t], ALU.add) \
                                .then_inc(sumsq_steps if h else half_summed, 1)
                            if h == 0:
                                dve.wait_ge(half_high, l + 2)
                                last_chunk_low(t, g)

                dve.wait_ge(std_ready, 2 * l + 2)
                dve.reciprocal(rbc[:, :], rbc[:, :]).then_inc(rbc_inverted, 1)
                dve.wait_ge(rbc_inverted, l + 1)
                hidden(0, 0)
                with dve.Fori(0, QUARTERS - 1) as q:
                    rest_of_quarter(q, False)
                    hidden(q, KC)
                rest_of_quarter(QUARTERS - 1, True)

            def last_rms(h):
                tiles = slice(h * NTOK // 2, (h + 1) * NTOK // 2)
                dve.wait_ge(std_ready, 2 * DEPTH + (h + 1))
                dve.reciprocal(rcol[:, tiles], rcol[:, tiles]).then_inc(rcol_ready, 1)
                dve.wait_ge(rcol_ready, DEPTH + (h + 1))
                for t in range(h * NTOK // 2, (h + 1) * NTOK // 2):
                    dve.tensor_scalar(diag[:, t, :], ident[:, :], rcol[:, t:t + 1], None, ALU.mult) \
                        .then_inc(diag_ready, 1)

            def finish(h, chunks):
                dve.wait_ge(rbc_ready, DEPTH + (h + 1))
                t = slice(h * HALF, (h + 1) * HALF)
                for m in chunks:
                    g = gain[:, 2 * DEPTH * KC + m:2 * DEPTH * KC + m + 1]
                    dve.scalar_tensor_tensor(final(m)[:, t], xt[:, m, t], g, rbc[:, t], ALU.mult, ALU.mult) \
                        .then_inc(out_ready, 1)

            last_rms(0)
            last_rms(1)
            finish(0, range(OUT_BY_POOL, KC))
            finish(1, range(OUT_BY_POOL, KC))


def kernel(**inputs):
    import numpy as np
    import concourse.bacc as bacc
    from concourse.bass_utils import run_bass_kernel_spmd as run

    a = {k: np.asarray(v) for k, v in inputs.items()}
    L = DEPTH
    qw, kvw, sw = HQ * HD, 2 * HD, GROUPS * HD
    rows = lambda w: w.reshape(L, KC, P, -1)
    tiles = lambda w: rows(w).reshape(L, KC, P, -1, P).transpose(0, 3, 2, 1, 4).reshape(L, -1, P, D)
    w_in = a["w_in"]
    q_cols = w_in[:, :, :qw].reshape(L, D, 2, 4, HD).transpose(0, 1, 3, 2, 4).reshape(L, D, qw)
    at = [qw, qw + kvw, qw + 2 * kvw, qw + 2 * kvw + sw, qw + 2 * kvw + 2 * sw]
    k_cols, v_cols, u_cols, gv_cols = (w_in[:, :, s:e] for s, e in zip(at, at[1:]))
    gv_part = rows(gv_cols).reshape(L, 4, 2, P, sw).transpose(0, 1, 3, 2, 4).reshape(L, 4, P, D)
    w_o = a["w_o"]
    att_rows = w_o[:, :qw].reshape(L, 2, 4, HD, D).transpose(0, 2, 1, 3, 4).reshape(L, qw, D)
    wo = np.concatenate([att_rows, w_o[:, qw:]], axis=1)
    up = tiles(a["w_up"]).reshape(L, QUARTERS, KC, P, D)
    down = a["w_down"].reshape(L, QUARTERS, KC, P, KC, P).transpose(0, 1, 4, 3, 2, 5).reshape(L, QUARTERS, KC, P, D)
    mlp = np.concatenate([up, down], axis=2).reshape(L, -1, P, D)
    stream = np.concatenate([gv_part, tiles(k_cols), tiles(q_cols), tiles(v_cols), tiles(u_cols), tiles(wo), mlp],
                            axis=1).reshape(L * PER_LAYER, P, D)
    norms = np.stack([a["norm_mix"][0], a["norm_ffn"][0], a["norm_mix"][1], a["norm_ffn"][1], a["norm_final"]])
    dist = np.abs(np.arange(CHUNK)[:, None] + CHUNK - np.arange(P)[None, :])
    alibi = np.zeros((2, CHUNK, 4, 2, P), np.float32)
    for c in range(4):
        for r in range(2):
            head = 4 * (c // 2) + 2 * (c % 2) + r
            alibi[r, :, c, 0] = alibi[r, :, c, 1] = -(2.0 ** (-8.0 * (head + 1) / HQ)) * dist
    alibi[:, :, :, 1, :CHUNK] = LOWEST
    arrays = {
        "x_in": a["x"][0].T.reshape(KC, P, SEQ),
        "gains_in": norms.reshape(5, KC, P).transpose(2, 0, 1).reshape(P, 5 * KC),
        "weights_in": stream,
        "sinks_in": a["sinks"].reshape(L, 4, 2).transpose(2, 0, 1),
        "ws_in": a["w_s"].transpose(0, 3, 1, 2),
        "bs_in": a["b_s"].reshape(L, 4, 2, P).transpose(2, 0, 1, 3),
        "alibi_in": alibi.reshape(P, 8 * P),
        "ident_in": np.eye(P, dtype=np.float32),
    }
    arrays = {k: np.ascontiguousarray(v) for k, v in arrays.items()}
    nc = bacc.Bacc("TRN2", target_bir_lowering=False, num_devices=1)
    ap = {k: nc.dram_tensor(k, v.shape, mybir.dt.from_np(v.dtype), kind="ExternalInput").ap()
          for k, v in arrays.items()}
    out = nc.dram_tensor("out_t", (KC, P, SEQ), F32, kind="ExternalOutput").ap()
    build(nc, ap["x_in"], ap["gains_in"], ap["weights_in"], ap["sinks_in"].rearrange("r l c -> l r c"), ap["ws_in"],
          ap["bs_in"].rearrange("r l c i -> l r c i"), ap["alibi_in"], ap["ident_in"], out)
    r = run(nc, [arrays], core_ids=[0])
    return np.ascontiguousarray(r.results[0]["out_t"].reshape(D, SEQ).T).reshape(1, SEQ, D)
```
